# Optimizing a Trainium2 kernel written in Bass

```python
import jax
import jax.numpy as jnp
from jax import lax
import numpy as np

D_MODEL = 1024
BATCH = 1
SEQ = 512
DEPTH = 4

N_MIXERS = 3
N_NSA = (DEPTH + 2) // 3
N_SGU = (DEPTH + 1) // 3
N_POOL = DEPTH // 3
RMS_EPS = 1e-6
LN_EPS = 1e-5
NEG_INF = -1e30
FORCE_SCORE = 1e9

NSA_HEADS = 16
NSA_KV_GROUPS = 4
NSA_HPG = NSA_HEADS // NSA_KV_GROUPS
NSA_HEAD_DIM = D_MODEL // NSA_HEADS
CMP_BLOCK = 32
CMP_STRIDE = 16
CMP_HIDDEN = 4 * NSA_HEAD_DIM
SEL_BLOCK = 64
SEL_TOPN = 16
WINDOW = 512
NSA_QBLOCK = 64
NSA_IN = NSA_HEADS * NSA_HEAD_DIM + 6 * NSA_KV_GROUPS * NSA_HEAD_DIM + 3 * NSA_HEADS
ROPE_THETA = 500000.0
ROPE_DIM = NSA_HEAD_DIM // 4

SGU_GROUPS = 8
SGU_WIDTH = D_MODEL
SGU_GROUP_DIM = SGU_WIDTH // SGU_GROUPS
SGU_CHUNK = 128

POOL_WINDOWS = (2, 4, 8, 16)
POOL_GROUPS = len(POOL_WINDOWS)
POOL_WIDTH = D_MODEL
POOL_GROUP_DIM = POOL_WIDTH // POOL_GROUPS

FFN_HIDDEN = -(-8 * D_MODEL // (3 * 256)) * 256

kernel_name = 'hybrid_nsa_gmlp_pool_swiglu_trunk'

def rmsnorm(x, g):
    xf = x.astype(jnp.float32)
    y = xf * lax.rsqrt(jnp.mean(xf * xf, axis=-1, keepdims=True) + RMS_EPS)
    return (y * g.astype(jnp.float32)).astype(x.dtype)

def layernorm(x, g, b):
    xf = x.astype(jnp.float32)
    mu = jnp.mean(xf, axis=-1, keepdims=True)
    var = jnp.mean(jnp.square(xf - mu), axis=-1, keepdims=True)
    y = (xf - mu) * lax.rsqrt(var + LN_EPS) * g.astype(jnp.float32) + b.astype(jnp.float32)
    return y.astype(x.dtype)

def rope_tables(positions):
    inv_freq = ROPE_THETA ** (-jnp.arange(0, ROPE_DIM, 2, dtype=jnp.float32) / ROPE_DIM)
    ang = positions.astype(jnp.float32)[..., None] * inv_freq
    return jnp.cos(ang)[:, None], jnp.sin(ang)[:, None]

def partial_rope(t, cos, sin):
    half = ROPE_DIM // 2
    tf = t[..., :ROPE_DIM].astype(jnp.float32)
    t1, t2 = tf[..., :half], tf[..., half:]
    rot = jnp.concatenate([t1 * cos - t2 * sin, t2 * cos + t1 * sin], axis=-1)
    return jnp.concatenate([rot.astype(t.dtype), t[..., ROPE_DIM:]], axis=-1)

def nsa_mixer(h, cos, sin, w_in, cmp_pos_k, cmp_k_w1, cmp_k_w2, cmp_pos_v, cmp_v_w1, cmp_v_w2, w_out):
    B, S, _ = h.shape
    H, G, P, dh, QB = NSA_HEADS, NSA_KV_GROUPS, NSA_HPG, NSA_HEAD_DIM, NSA_QBLOCK
    splits = [H * dh + k * G * dh for k in range(7)]
    q, kc, vc, ks, vs, kw, vw, gl = jnp.split(h @ w_in, splits, axis=-1)

    def to_heads(t, n):
        return t.reshape(B, S, n, dh).transpose(0, 2, 1, 3)

    q = (partial_rope(to_heads(q, H), cos, sin) * (dh ** -0.5)).reshape(B, G, P, S, dh)
    kc, ks, kw = [partial_rope(to_heads(t, G), cos, sin) for t in (kc, ks, kw)]
    vc, vs, vw = [to_heads(t, G) for t in (vc, vs, vw)]
    gates = jax.nn.sigmoid(gl.astype(jnp.float32)).astype(h.dtype)
    gates = gates.reshape(B, S, 3, G, P).transpose(0, 2, 3, 4, 1)

    n_cmp = (S - CMP_BLOCK) // CMP_STRIDE + 1
    cmp_start = jnp.arange(n_cmp) * CMP_STRIDE
    cmp_end = cmp_start + CMP_BLOCK - 1
    tok_idx = cmp_start[:, None] + jnp.arange(CMP_BLOCK)[None, :]

    def compress(t, pos, w1, w2):
        blk = (t[:, :, tok_idx, :] + pos).reshape(B, G, n_cmp, CMP_BLOCK * dh)
        return jax.nn.gelu(blk @ w1) @ w2

    k_cmp = compress(kc, cmp_pos_k, cmp_k_w1, cmp_k_w2)
    v_cmp = compress(vc, cmp_pos_v, cmp_v_w1, cmp_v_w2)

    n_sel = S // SEL_BLOCK
    n_top = min(SEL_TOPN, n_sel)
    sel_ids = jnp.arange(n_sel)
    sel_start = sel_ids * SEL_BLOCK
    overlap = ((cmp_start[:, None] <= sel_start[None, :] + SEL_BLOCK - 1)
               & (cmp_end[:, None] >= sel_start[None, :])).astype(jnp.float32)
    ks_blk = ks.reshape(B, G, n_sel, SEL_BLOCK, dh)
    vs_blk = vs.reshape(B, G, n_sel, SEL_BLOCK, dh)
    b_idx = jnp.arange(B)[:, None, None, None]
    g_idx = jnp.arange(G)[None, :, None, None]

    kw_pad = jnp.pad(kw, ((0, 0), (0, 0), (WINDOW, 0), (0, 0)))
    vw_pad = jnp.pad(vw, ((0, 0), (0, 0), (WINDOW, 0), (0, 0)))

    def block_fn(bi):
        s = bi * QB
        qb = lax.dynamic_slice_in_dim(q, s, QB, axis=3)
        t_pos = s + jnp.arange(QB)

        sc = jnp.einsum('bgpqd,bgnd->bgpqn', qb, k_cmp).astype(jnp.float32)
        valid_c = cmp_end[None, :] <= t_pos[:, None]
        p_c = jax.nn.softmax(jnp.where(valid_c, sc, NEG_INF), axis=-1)
        p_c = jnp.where(valid_c.any(-1)[:, None], p_c, 0.0)
        o_c = jnp.einsum('bgpqn,bgnd->bgpqd', p_c.astype(v_cmp.dtype), v_cmp)

        imp = jnp.einsum('bgpqn,nm->bgqm', p_c, overlap)
        cur = (t_pos // SEL_BLOCK)[:, None]
        forced = (sel_ids[None, :] == 0) | (sel_ids[None, :] == cur) | (sel_ids[None, :] == cur - 1)
        imp = jnp.where(forced, FORCE_SCORE, imp)
        imp = jnp.where(sel_start[None, :] <= t_pos[:, None], imp, NEG_INF)
        _, sel_idx = lax.top_k(imp, n_top)
        k_sel = ks_blk[b_idx, g_idx, sel_idx]
        v_sel = vs_blk[b_idx, g_idx, sel_idx]
        key_pos = sel_idx[..., None] * SEL_BLOCK + jnp.arange(SEL_BLOCK)
        valid_s = key_pos <= t_pos[None, None, :, None, None]
        ss = jnp.einsum('bgpqd,bgqnld->bgpqnl', qb, k_sel).astype(jnp.float32)
        ss = jnp.where(valid_s[:, :, None], ss, NEG_INF)
        p_s = jax.nn.softmax(ss.reshape(B, G, P, QB, n_top * SEL_BLOCK), axis=-1)
        p_s = p_s.reshape(B, G, P, QB, n_top, SEL_BLOCK).astype(v_sel.dtype)
        o_s = jnp.einsum('bgpqnl,bgqnld->bgpqd', p_s, v_sel)

        kwb = lax.dynamic_slice_in_dim(kw_pad, s, WINDOW + QB, axis=2)
        vwb = lax.dynamic_slice_in_dim(vw_pad, s, WINDOW + QB, axis=2)
        kpos = s - WINDOW + jnp.arange(WINDOW + QB)
        rel = t_pos[:, None] - kpos[None, :]
        valid_w = (rel >= 0) & (rel < WINDOW) & (kpos[None, :] >= 0)
        sw = jnp.einsum('bgpqd,bgkd->bgpqk', qb, kwb).astype(jnp.float32)
        p_w = jax.nn.softmax(jnp.where(valid_w, sw, NEG_INF), axis=-1).astype(vwb.dtype)
        o_w = jnp.einsum('bgpqk,bgkd->bgpqd', p_w, vwb)

        gb = lax.dynamic_slice_in_dim(gates, s, QB, axis=4)[..., None]
        o = gb[:, 0] * o_c + gb[:, 1] * o_s + gb[:, 2] * o_w
        return o.astype(h.dtype)

    out = lax.map(block_fn, jnp.arange(S // QB))
    out = out.transpose(1, 0, 4, 2, 3, 5).reshape(B, S, H * dh)
    return out @ w_out

def sgu_mixer(h, w_in, ln_g, ln_b, w_s, b_s, w_out):
    B, S, _ = h.shape
    T = SGU_CHUNK
    u, v = jnp.split(jax.nn.gelu(h @ w_in), 2, axis=-1)
    v = layernorm(v, ln_g, ln_b).reshape(B, S // T, T, SGU_GROUPS, SGU_GROUP_DIM)
    ws = jnp.where(jnp.tril(jnp.ones((T, T), dtype=bool)), w_s, 0.0)
    sv = jnp.einsum('gts,bnsgc->bntgc', ws, v) + b_s.T[None, None, :, :, None]
    return (u * sv.reshape(B, S, SGU_WIDTH).astype(u.dtype)) @ w_out

def pool_mixer(h, w_in, w_grp, scale, w_out):
    B, S, _ = h.shape
    z = (h @ w_in).astype(jnp.float32)
    csum = jnp.pad(jnp.cumsum(z, axis=1), ((0, 0), (1, 0), (0, 0)))
    t = jnp.arange(S)
    diffs = []
    for gi, w in enumerate(POOL_WINDOWS):
        sl = slice(gi * POOL_GROUP_DIM, (gi + 1) * POOL_GROUP_DIM)
        lo = jnp.maximum(t + 1 - w, 0)
        win = csum[:, 1:, sl] - csum[:, lo, sl]
        cnt = (t + 1 - lo).astype(jnp.float32)[None, :, None]
        diffs.append(win / cnt - z[..., sl])
    d = jnp.stack(diffs, axis=2)
    y = jnp.einsum('bsgc,gce->bsge', d, w_grp.astype(jnp.float32)).reshape(B, S, POOL_WIDTH)
    y = y * scale.astype(jnp.float32)
    return y.astype(h.dtype) @ w_out

def swiglu(h, w_gate_up, w_down):
    g, u = jnp.split(h @ w_gate_up, 2, axis=-1)
    return (jax.nn.silu(g) * u) @ w_down

def setup_inputs(seed: int = 0) -> dict:
    key = jax.random.key(seed)
    keys = iter(jax.random.split(key, 32))

    def nrm(shape, scale):
        return scale * jax.random.normal(next(keys), shape, jnp.float32)

    D, dh, G = D_MODEL, NSA_HEAD_DIM, NSA_KV_GROUPS
    res = (2 * DEPTH) ** -0.5
    x = jax.random.normal(next(keys), (BATCH, SEQ, D), jnp.float32)
    positions = (jnp.arange(SEQ, dtype=jnp.int32)[None, :]
                 + jax.random.randint(next(keys), (BATCH, 1), 0, 1024, dtype=jnp.int32))
    return {
        'x': x,
        'positions': positions,
        'mix_norm': 1.0 + nrm((DEPTH, D), 0.05),
        'ffn_norm': 1.0 + nrm((DEPTH, D), 0.05),
        'final_norm': 1.0 + nrm((D,), 0.05),
        'nsa_w_in': nrm((N_NSA, D, NSA_IN), D ** -0.5),
        'nsa_cmp_pos_k': nrm((N_NSA, CMP_BLOCK, dh), 0.1),
        'nsa_cmp_k_w1': nrm((N_NSA, CMP_BLOCK * dh, CMP_HIDDEN), (CMP_BLOCK * dh) ** -0.5),
        'nsa_cmp_k_w2': nrm((N_NSA, CMP_HIDDEN, dh), CMP_HIDDEN ** -0.5),
        'nsa_cmp_pos_v': nrm((N_NSA, CMP_BLOCK, dh), 0.1),
        'nsa_cmp_v_w1': nrm((N_NSA, CMP_BLOCK * dh, CMP_HIDDEN), (CMP_BLOCK * dh) ** -0.5),
        'nsa_cmp_v_w2': nrm((N_NSA, CMP_HIDDEN, dh), CMP_HIDDEN ** -0.5),
        'nsa_w_out': nrm((N_NSA, NSA_HEADS * dh, D), res * (NSA_HEADS * dh) ** -0.5),
        'sgu_w_in': nrm((N_SGU, D, 2 * SGU_WIDTH), D ** -0.5),
        'sgu_ln_g': 1.0 + nrm((N_SGU, SGU_WIDTH), 0.05),
        'sgu_ln_b': nrm((N_SGU, SGU_WIDTH), 0.02),
        'sgu_w_s': nrm((N_SGU, SGU_GROUPS, SGU_CHUNK, SGU_CHUNK), SGU_CHUNK ** -0.5),
        'sgu_b_s': 1.0 + nrm((N_SGU, SGU_GROUPS, SGU_CHUNK), 0.1),
        'sgu_w_out': nrm((N_SGU, SGU_WIDTH, D), res * SGU_WIDTH ** -0.5),
        'pool_w_in': nrm((N_POOL, D, POOL_WIDTH), D ** -0.5),
        'pool_w_grp': nrm((N_POOL, POOL_GROUPS, POOL_GROUP_DIM, POOL_GROUP_DIM), POOL_GROUP_DIM ** -0.5),
        'pool_scale': 1.0 + nrm((N_POOL, POOL_WIDTH), 0.1),
        'pool_w_out': nrm((N_POOL, POOL_WIDTH, D), res * POOL_WIDTH ** -0.5),
        'ffn_w_gate_up': nrm((DEPTH, D, 2 * FFN_HIDDEN), D ** -0.5),
        'ffn_w_down': nrm((DEPTH, FFN_HIDDEN, D), res * FFN_HIDDEN ** -0.5),
    }

def reference(x, positions, mix_norm, ffn_norm, final_norm,
              nsa_w_in, nsa_cmp_pos_k, nsa_cmp_k_w1, nsa_cmp_k_w2,
              nsa_cmp_pos_v, nsa_cmp_v_w1, nsa_cmp_v_w2, nsa_w_out,
              sgu_w_in, sgu_ln_g, sgu_ln_b, sgu_w_s, sgu_b_s, sgu_w_out,
              pool_w_in, pool_w_grp, pool_scale, pool_w_out,
              ffn_w_gate_up, ffn_w_down):
    cos, sin = rope_tables(positions)
    for i in range(DEPTH):
        kind, j = i % N_MIXERS, i // N_MIXERS
        h = rmsnorm(x, mix_norm[i])
        if kind == 0:
            m = nsa_mixer(h, cos, sin, nsa_w_in[j], nsa_cmp_pos_k[j], nsa_cmp_k_w1[j], nsa_cmp_k_w2[j],
                          nsa_cmp_pos_v[j], nsa_cmp_v_w1[j], nsa_cmp_v_w2[j], nsa_w_out[j])
        elif kind == 1:
            m = sgu_mixer(h, sgu_w_in[j], sgu_ln_g[j], sgu_ln_b[j], sgu_w_s[j], sgu_b_s[j], sgu_w_out[j])
        else:
            m = pool_mixer(h, pool_w_in[j], pool_w_grp[j], pool_scale[j], pool_w_out[j])
        x = x + m
        x = x + swiglu(rmsnorm(x, ffn_norm[i]), ffn_w_gate_up[i], ffn_w_down[i])
    return rmsnorm(x, final_norm)


_drawn_inputs = setup_inputs


def setup_inputs(seed=0):
    import zlib

    import numpy as np

    out = dict(_drawn_inputs(seed))
    spreads = {}
    factors = {'nsa_cmp_pos_k': 30.864,
     'nsa_cmp_pos_v': 3.694,
     'sgu_ln_g': 6.915,
     'sgu_ln_b': 28.041,
     'sgu_b_s': 3.498,
     'pool_scale': 3.082}
    for name, (base, spread) in spreads.items():
        noise = np.random.default_rng([zlib.crc32(name.encode()), seed]).standard_normal(out[name].shape)
        drawn = base * np.exp(spread * noise) if base else spread * noise
        out[name] = jnp.asarray(drawn.astype(out[name].dtype))
    for name, factor in factors.items():
        out[name] = (out[name] * factor).astype(out[name].dtype)
    return out
```

```python
from contextlib import ExitStack

import numpy as np

import concourse.bass as bass
from concourse import mybir

F32 = mybir.dt.float32
F32R = mybir.dt.float32r
BF16 = mybir.dt.bfloat16
I32 = mybir.dt.int32
ALU = mybir.AluOpType
ACT = mybir.ActivationFunctionType
AX = mybir.AxisListType

P = 128
S = 512
D = 1024
MT = D // P
TT = S // P
HEADS, GROUPS, DH = 16, 4, 64
NCMP = 32
HIDDEN_TILES = 22
PARTS = (8, 8, 6)
BW = 1024
RING = 4
RAW = 2
AHEAD = RING - 1
KCW = S + 16
VW = DH + 2
POOL_PAD = 16
RMS_EPS, LN_EPS, NEG = 1e-6, 1e-5, -1e30
ROPE_THETA, ROPE_DIM = 500000.0, 16

MIXERS = (("nsa", 0), ("sgu", 0), ("pool", 0), ("nsa", 1))
MIX_BLOCKS = {"nsa": 38, "sgu": 25, "pool": 18}
FFN_BLOCKS = 2 * HIDDEN_TILES + MT * len(PARTS)

(KC, VC, KS, KWIN, W1K, W1V, W2, Q, GATE, V, NSA_OUT) = (0, 2, 4, 6, 8, 12, 16, 17, 25, 26, 30)
SGU_V, SGU_WS, SGU_U, SGU_OUT = 0, 8, 9, 17
POOL_Z, POOL_GRP, POOL_OUT = 0, 8, 10

TWO_PI = (6.28125, 0.0019340515136718750, 1.2556659146e-6)
ROUND = 1.5 * 2.0 ** 23
PI_F = 3.1415925
ROPE_STEPS = 13

PAR = {}
_at = 0
for _name, _n in (("gn", 9 * MT), ("ln_g", MT), ("ln_b", MT), ("pool_scale", MT), ("pos", 2 * 2 * 16),
                  ("invf", 1), ("anyvalid", 1), ("corr", 4 * POOL_PAD)):
    PAR[_name] = _at
    _at += _n
PAR_COLS = _at
CON = {"ident": 0, "swap": 128, "causal": 256, "tril": 384, "cmask": 512, "blk": 512 + TT * P}
CON_COLS = CON["blk"] + 4


class Plan:

    def __init__(self, mixers):
        self.mixers = mixers
        self.mix, self.ffn, self.nsa = [], [], []
        b = a = 0
        for kind, _ in mixers:
            self.mix.append(b)
            self.nsa.append(a)
            a += kind == "nsa"
            b += MIX_BLOCKS[kind]
            self.ffn.append(b)
            b += FFN_BLOCKS
        self.blocks = b
        self.stream = b + AHEAD + (b + AHEAD) % 2
        self.norms = 2 * len(mixers) + 1

    def out_block(self, l):
        kind = self.mixers[l][0]
        return self.mix[l] + {"nsa": NSA_OUT, "sgu": SGU_OUT, "pool": POOL_OUT}[kind]

    def part_block(self, l, p):
        up = self.ffn[l] + sum(2 * n + MT for n in PARTS[:p])
        return up, up + 2 * PARTS[p]

    def norm_blocks(self, n):
        return self.out_block(n // 2) if n % 2 else self.part_block(n // 2 - 1, 2)[1]


def build(nc, x_in, positions, stream, params, consts, b_s, out, mixers=MIXERS):
    plan = Plan(mixers)
    ctx = ExitStack()
    with ctx:
        def sb(name, shape, dt):
            return ctx.enter_context(nc.sbuf_tensor(name, shape, dt))

        def sem(name):
            return ctx.enter_context(nc.semaphore(name))

        x = sb("x", [P, MT, S], F32)
        xs_hi = sb("xs_hi", [P, MT * S + 64], F32R)
        xs_lo = sb("xs_lo", [P, MT, S], F32R)
        raw = sb("raw", [P, RAW, BW], F32)
        w_hi = sb("w_hi", [P, RING, BW], F32R)
        w_lo = sb("w_lo", [P, RING, BW], F32R)
        hid_hi = sb("hid_hi", [P, MT, S], F32R)
        hid_lo = sb("hid_lo", [P, MT, S], F32R)
        mix_hi = sb("mix_hi", [P, MT, S], F32R)
        mix_lo = sb("mix_lo", [P, MT, S], F32R)
        big = sb("big", [P, 2 * GROUPS * KCW], F32)
        tmp = sb("tmp", [P, 4, S], F32)
        rstat = sb("rstat", [P, S + 2 * TT], F32)
        vstat = sb("vstat", [P, S + 2 * TT], F32)
        work = sb("work", [P, 2, S], F32)
        work2 = sb("work2", [P, 2, S], F32)
        rope = sb("rope", [P, 2, S], F32)
        sm_hi = sb("sm_hi", [P, GROUPS, 4 * DH], F32R)
        sm_lo = sb("sm_lo", [P, GROUPS, 4 * DH], F32R)
        par = sb("par", [P, PAR_COLS], F32)
        ident = sb("ident", [P, P], F32)
        tril = sb("tril", [P, P], BF16)
        ones = sb("ones", [P, P], F32R)
        swap = sb("swap", [P, P], F32R)
        ident_b = sb("ident_b", [P, P], BF16)
        causal_b = sb("causal_b", [P, P], BF16)
        blk = sb("blk", [P, 4], F32R)
        cmask_b = sb("cmask_b", [P, TT, P], BF16)
        kc_hi = sb("kc_hi", [P, P], F32R)
        kc_lo = sb("kc_lo", [P, P], F32R)
        vc_hi = sb("vc_hi", [P, DH], F32R)
        vc_lo = sb("vc_lo", [P, DH], F32R)
        gates = sb("gates", [P, TT, 3, HEADS], F32)
        nmax = sb("nmax", [P, 4, 4], F32)
        den = sb("den", [P, 3, 4], F32)
        wgt = sb("wgt", [P, 3, 4], F32)
        bnst = sb("bnst", [P, TT, 2, 6], F32)
        mv = sb("mv", [P, TT, 2], F32)
        lstd = sb("lstd", [P, 4, TT], F32)

        bank = [ctx.enter_context(nc.psum_tensor(f"bank{i}", [P, S], F32)) for i in range(8)]

        xh = xs_hi[:, 0:MT * S].rearrange("p (m t) -> p m t", m=MT)
        val_hi = xs_hi[:, 0:TT * 8 * VW].rearrange("p (t n c) -> p t n c", t=TT, n=8)
        val_lo = xs_hi[:, TT * 8 * VW:TT * 8 * (VW + DH)].rearrange("p (t n c) -> p t n c", t=TT, n=8)
        q_st = xs_lo[:, 0:4, :]
        pt_hi = xs_lo[:, 4:6, :]
        pt_lo = xs_lo[:, 6:8, :]
        key_hi = hid_hi[:, :, :].rearrange("p (r g) t -> p r g t", r=2)
        key_lo = hid_lo[:, :, :].rearrange("p (r g) t -> p r g t", r=2)
        cm_hi = mix_hi[:, :, :].rearrange("p (v k) t -> p v (k t)", v=2)
        cm_lo = mix_lo[:, :, :].rearrange("p (v k) t -> p v (k t)", v=2)
        kc2 = big[:, :].rearrange("p (v g t) -> p v g t", v=2, g=GROUPS)
        qf = big[:, 0:MT * S].rearrange("p (m t) -> p m t", m=MT)
        sgu_v = big[:, 0:TT * D].rearrange("p (t c) -> p t c", t=TT)
        sq_hi = sm_hi[:, 0:2, :].rearrange("p a b -> p (a b)")
        sq_lo = sm_lo[:, 0:2, :].rearrange("p a b -> p (a b)")
        ch_hi = sm_hi[:, 2:4, :].rearrange("p a (b n) -> p (a b) n", b=2)
        ch_lo = sm_lo[:, 2:4, :].rearrange("p a (b n) -> p (a b) n", b=2)
        vc_f = tmp[:, 3, 0:DH]
        ws_hi = sm_hi[:, :, :].rearrange("p a b -> p (a b)")
        ws_lo = sm_lo[:, :, :].rearrange("p a b -> p (a b)")
        bias_t = work[:, :, :].rearrange("p a b -> p (a b)")
        bs_t = work2[:, :, :].rearrange("p a b -> p (a b)")
        v_hi = hid_hi[:, :, :].rearrange("p m t -> p (m t)").rearrange("p (t c) -> p t c", t=TT)
        v_lo = hid_lo[:, :, :].rearrange("p m t -> p (m t)").rearrange("p (t c) -> p t c", t=TT)
        con = big[:, 0:CON_COLS]
        rrow, rcol = rstat[:, 0:S], rstat[:, S:S + 2 * TT].rearrange("p (t c) -> p t c", c=2)

        def f32(ap):
            return ap.bitcast(F32)

        def tile(t, m):
            return t[:, m, :] if type(m) is int else t[:, bass.ds(m, 1), :].rearrange("p o t -> p (o t)")

        def g_of(n, m):
            return par[:, bass.ds(PAR["gn"] + n * MT + m, 1)]

        def col(name, i):
            return par[:, PAR[name] + i:PAR[name] + i + 1]

        raw_full = [sem(f"raw_full{i}") for i in range(RAW)]
        par_full, con_full, pos_full, x_full, bs_full = (sem(n) for n in (
            "par_full", "con_full", "pos_full", "x_full", "bs_full"))
        out_done = sem("out_done")
        w_hi_ready, w_lo_ready = sem("w_hi_ready"), sem("w_lo_ready")
        block_done = sem("block_done")
        taken = sem("taken")
        xs_hi_ready, xs_lo_ready = sem("xs_hi_ready"), sem("xs_lo_ready")
        sq_step, sumsq_ready = sem("sq_step"), sem("sumsq_ready")
        sq_hi_ready, sq_lo_ready = sem("sq_hi_ready"), sem("sq_lo_ready")
        norm_sum, var_ready, std_ready, norm_step = (sem(n) for n in (
            "norm_sum", "var_ready", "std_ready", "norm_step"))
        silu_ready, hid_full = sem("silu_ready"), sem("hid_full")
        hid_hi_ready, hid_lo_ready = sem("hid_hi_ready"), sem("hid_lo_ready")
        con_ready, ones_ready, rope_step, rope_sin = (sem(n) for n in (
            "con_ready", "ones_ready", "rope_step", "rope_sin"))
        tab_ready = sem("tab_ready")
        rq_hi_ready, rq_lo_ready, swapped, rot_b, rotated = (sem(n) for n in (
            "rq_hi_ready", "rq_lo_ready", "swapped", "rot_b", "rotated"))
        kc_rows, key_hi_ready, key_lo_ready = sem("kc_rows"), sem("key_hi_ready"), sem("key_lo_ready")
        kc_pad = sem("kc_pad")
        cm_full, cm_hi_ready, cm_lo_ready = sem("cm_full"), sem("cm_hi_ready"), sem("cm_lo_ready")
        ch_full, ch_hi_ready = sem("ch_full"), sem("ch_hi_ready")
        kcmp_hi, vcmp_full, vcmp_hi, vcmp_lo = (sem(n) for n in ("kcmp_hi", "vcmp_full", "vcmp_hi", "vcmp_lo"))
        vcb_zero, vcb_hi, vcb_lo, val_ones, val_hi_ready = (sem(n) for n in (
            "vcb_zero", "vcb_hi", "vcb_lo", "val_ones", "val_hi_ready"))
        gate_ready = sem("gate_ready")
        q_hi_ready, q_lo_ready = sem("q_hi_ready"), sem("q_lo_ready")
        score_ready, max_ready, prob_ready, prob_t, pt_hi_ready, pt_lo_ready, pv_done = (sem(n) for n in (
            "score_ready", "max_ready", "prob_ready", "prob_t", "pt_hi_ready", "pt_lo_ready", "pv_done"))
        cmax_ready = sem("cmax_ready")
        o_step, den_step, o_sum, o_full, ot_ready, ot_hi_ready, ot_lo_ready = (sem(n) for n in (
            "o_step", "den_step", "o_sum", "o_full", "ot_ready", "ot_hi_ready", "ot_lo_ready"))
        v_gelu, ln_step, ln_var, ln_std, vn_ready, vn_hi, vn_lo = (sem(n) for n in (
            "v_gelu", "ln_step", "ln_var", "ln_std", "vn_ready", "vn_hi", "vn_lo"))
        ws_masked, bias_ready, u_gelu, mixed, sv_ready, mix_full, mix_hi_ready, mix_lo_ready = (
            sem(n) for n in ("ws_masked", "bias_ready", "u_gelu", "mixed", "sv_ready", "mix_full",
                             "mix_hi_ready", "mix_lo_ready"))
        pool_step, d_full, d_hi, d_lo, y_hi, y_lo, z_pad = (sem(n) for n in (
            "pool_step", "d_full", "d_hi", "d_lo", "y_hi", "y_lo", "z_pad"))
        y_out = sem("y_out")

        norm_of_mixer = lambda l: 2 * l
        norm_of_ffn = lambda l: 2 * l + 1

        def wait_past(eng, sem_, value):
            if not (type(value) is int and value <= 0):
                eng.wait_ge(sem_, value)

        def wait_x(eng, n, m):
            if n == 0:
                eng.wait_ge(x_full, 16)
            else:
                eng.wait_ge(taken, plan.norm_blocks(n) + m + 1)

        block = ctx.enter_context(nc.Block())

        @block.sync
        def _(sp):
            sp.dma_start(par[:, :], params).then_inc(par_full, 16)
            sp.dma_start(x[:, :, :], x_in).then_inc(x_full, 16)
            for k in range(RAW):
                sp.dma_start(raw[:, k, :], stream[k]).then_inc(raw_full[k], 16)
            sp.dma_start(con, consts).then_inc(con_full, 16)
            sp.dma_start(tmp[:, 0, :].bitcast(I32), positions.partition_broadcast(P)).then_inc(pos_full, 16)

            def load(b, k):
                sp.wait_ge(w_lo_ready, b - RAW + 1)
                sp.dma_start(raw[:, k, :], stream[b]).then_inc(raw_full[k], 16)

            with sp.Fori(1, plan.stream // RAW) as i:
                for k in range(RAW):
                    load(i * RAW + k, k)
            for m in range(MT):
                sp.wait_ge(y_out, m + 1)
                sp.dma_start(out[:, m, :], qf[:, m, :]).then_inc(out_done, 16)
            sp.wait_ge(out_done, 16 * MT)

        @block.gpsimd
        def _(gp):
            def squares(n):
                base = (2 * MT - 1) * n
                wait_x(gp, n, 0)
                if n:
                    gp.wait_ge(norm_step, 5 * n)
                gp.tensor_tensor(work[:, 0, :], x[:, 0, :], x[:, 0, :], ALU.mult).then_inc(sq_step, 1)
                with gp.Fori(1, MT) as m:
                    wait_x(gp, n, m)
                    gp.wait_ge(sq_step, 2 * m + base - 1)
                    gp.tensor_tensor(work2[:, 0, :], tile(x, m), tile(x, m), ALU.mult).then_inc(sq_step, 1)
                    gp.wait_ge(sq_step, 2 * m + base)
                    gp.tensor_tensor(work[:, 0, :], work[:, 0, :], work2[:, 0, :], ALU.add).then_inc(sq_step, 1)

            def nsa(l, a):
                gp.wait_ge(block_done, plan.mix[l] + GATE)
                gp.wait_ge(swapped, 14 * (a + 1))
                gp.memset(sm_hi[:, :, :].bitcast(F32), 0.0).then_inc(vcb_zero, 1)
                gp.memset(sm_lo[:, :, :].bitcast(F32), 0.0).then_inc(vcb_zero, 1)
                def group(g):
                    for t in range(TT):
                        e = g * TT + (16 * a + t)
                        gp.wait_ge(o_step, 3 * e + 2)
                        gp.tensor_tensor(tmp[:, 3, 0:256], work[:, 0, 0:256], work[:, 0, 256:512], ALU.add
                                         ).then_inc(o_sum, 1)
                        gp.wait_ge(o_sum, e + 1)
                        gp.wait_ge(o_step, 3 * e + 3)
                        wait_past(gp, ot_ready, e)
                        gp.tensor_tensor(work2[:, 0, 0:256], tmp[:, 3, 0:256], work[:, 1, 0:256], ALU.add
                                         ).then_inc(o_full, 1)

                if a == 0:
                    group(0)
                with gp.Fori(1 if a == 0 else 0, GROUPS) as g:
                    group(g)

            squares(0)
            a = 0
            for l, (kind, _) in enumerate(plan.mixers):
                if kind == "nsa":
                    nsa(l, a)
                    a += 1
                squares(norm_of_ffn(l))
                squares(norm_of_ffn(l) + 1)

        @block.scalar
        def _(act):
            def split(b, slot=None):
                slot = b % RING if slot is None else slot
                k = slot % RAW
                nth = (b - k) // RAW if type(b) is int else None
                act.wait_ge(raw_full[k], 16 * (nth + 1) if nth is not None else (b - k) * 8 + 16)
                if not (type(b) is int and b < RING):
                    act.wait_ge(block_done, b - RING + 1)
                nc.scalar.activation(w_hi[:, slot, :], raw[:, k, :], ACT.Copy).then_inc(w_hi_ready, 1)

            def split_after(b, slot):
                split(b + AHEAD, (slot + AHEAD) % RING)

            def xs_high(n, m):
                wait_x(act, n, m)
                nc.scalar.activation(tile(xh, m), tile(x, m), ACT.Copy, scale=g_of(n, m)).then_inc(xs_hi_ready, 1)

            def sum_split(n):
                act.wait_ge(sq_step, (2 * MT - 1) * (n + 1))
                nc.scalar.activation(sq_hi, work[:, 0, :], ACT.Copy).then_inc(sq_hi_ready, 1)

            def root(n):
                act.wait_ge(var_ready, 2 * (n + 1))
                nc.scalar.activation(rstat[:, :], vstat[:, :], ACT.Sqrt).then_inc(std_ready, 1)

            def residual(n, b, slot):
                split_after(b, slot)

            def out_projection(l):
                n, b0 = norm_of_ffn(l), plan.out_block(l)
                s0 = b0 % RING
                with act.Fori(0, MT // RING) as i:
                    for k in range(RING):
                        split_after(i * RING + (b0 + k), (s0 + k) % RING)
                        xs_high(n, i * RING + k)

            def ffn(l):
                n = norm_of_ffn(l)

                def hidden_tile(t, b, slot, first=False):
                    split_after(b, slot)
                    if first:
                        root(n)
                    act.wait_ge(taken, b + 1)
                    nc.scalar.activation(tmp[:, 1, :], tmp[:, 0, :], ACT.Silu).then_inc(silu_ready, 1)
                    split_after(b + 1, (slot + 1) % RING)
                    act.wait_ge(hid_full, t + 1)

                for p, tiles in enumerate(PARTS):
                    up, down = plan.part_block(l, p)
                    s0 = up % RING
                    t0 = HIDDEN_TILES * l + 8 * p

                    def pair(i):
                        for k in range(2):
                            hidden_tile(i * 2 + (t0 + k), i * 4 + (up + 2 * k), (s0 + 2 * k) % RING,
                                 p == 0 and k == 0 and type(i) is int)
                            nc.scalar.activation(hid_hi[:, bass.ds(i * 2 + k, 1), :], tmp[:, 3:4, :], ACT.Copy
                                                 ).then_inc(hid_hi_ready, 1)

                    first = 0
                    if p == 0:
                        sum_split(n)
                        pair(0)
                        first = 1
                    with act.Fori(first, tiles // 2) as i:
                        pair(i)
                    s0d = down % RING
                    with act.Fori(0, MT // RING) as i:
                        for k in range(RING):
                            split_after(i * RING + (down + k), (s0d + k) % RING)
                            if p == len(PARTS) - 1 and n + 1 < plan.norms - 1:
                                xs_high(n + 1, i * RING + k)

            def rope_high(b, slot, rho):
                act.wait_ge(block_done, b + 1)
                if not (type(rho) is int and rho == 0):
                    act.wait_ge(swapped, rho)
                nc.scalar.activation(sm_hi[:, 0:2, :].rearrange("p a b -> p (a b)"), bank[slot][:, :], ACT.Copy
                                     ).then_inc(rq_hi_ready, 1)

            def nsa(l, a):
                B = plan.mix[l]
                n = norm_of_mixer(l)

                def post(j):
                    rt = tmp[:, j % 2, :]
                    if j in (VC, VC + 1):
                        act.wait_ge(taken, B + j + 1)
                    else:
                        rho = j if j < 2 else j - 2
                        act.wait_ge(rotated, 14 * a + rho + 1)
                    for half in range(2):
                        g = 2 * (j % 2) + half
                        src = rt[64 * half:64 * half + 64, :]
                        if j < KS:
                            if half == 0 and j == 0:
                                act.wait_ge(kc_pad, 2 * (a + 1))
                            v = j // 2
                            nc.scalar.activation(kc2[0:64, v, g, 0:S], src, ACT.Copy).then_inc(kc_rows, 1)
                            nc.scalar.activation(kc2[64:128, v, g, 0:S - 1], src[:, 1:S], ACT.Copy
                                                 ).then_inc(kc_rows, 1)
                        else:
                            r = (j - KS) // 2
                            for h in (half, 1 - half):
                                nc.scalar.activation(key_hi[64 * h:64 * h + 64, r, g, :], src, ACT.Copy
                                                     ).then_inc(key_hi_ready, 1)

                def cm_high(c):
                    act.wait_ge(cm_full, 8 * a + c + 1)
                    nc.scalar.activation(cm_hi[:, c // 4, bass.ts(c % 4, S)], tmp[:, 3, :], ACT.Copy
                                         ).then_inc(cm_hi_ready, 1)

                sum_split(n)
                for j in range(W1K):
                    b, slot = B + j, (B + j) % RING
                    split_after(b, slot)
                    if j == 0:
                        root(n)
                    if j not in (VC, VC + 1):
                        rope_high(b, slot, 14 * a + (j if j < 2 else j - 2))
                    if j:
                        post(j - 1)
                    if j >= 4:
                        cm_high(j - 4)
                post(W1K - 1)
                for j in range(W1K, W2):
                    b, slot = B + j, (B + j) % RING
                    split_after(b, slot)
                    if j < W1K + 4:
                        cm_high(j - W1K + 4)
                    if j % 2:
                        q = (j - W1K) // 2
                        act.wait_ge(block_done, b + 1)
                        nc.scalar.activation(tmp[:, 2, bass.ts(q, P)], bank[(slot - 1) % RING][:, 0:P],
                                             ACT.Gelu_apprx_tanh).then_inc(ch_full, 1)
                        act.wait_ge(ch_full, 4 * a + q + 1)
                        nc.scalar.activation(ch_hi[:, q, :], tmp[:, 2, bass.ts(q, P)], ACT.Copy
                                             ).then_inc(ch_hi_ready, 1)
                b, slot = B + W2, (B + W2) % RING
                split_after(b, slot)
                act.wait_ge(block_done, b + 1)
                nc.scalar.activation(kc_hi[:, :], bank[slot][:, 0:P], ACT.Copy).then_inc(kcmp_hi, 1)
                nc.scalar.activation(vc_f, bank[6][:, 0:DH], ACT.Copy).then_inc(vcmp_full, 1)
                act.wait_ge(vcmp_full, a + 1)
                nc.scalar.activation(vc_hi[:, :], vc_f, ACT.Copy).then_inc(vcmp_hi, 1)

                with act.Fori(0, 2) as i:
                    for k in range(RING):
                        slot = (B + Q + k) % RING
                        b = i * RING + (B + Q + k)
                        split_after(b, slot)
                        rope_high(b, slot, i * RING + (14 * a + 6 + k))
                b, slot = B + GATE, (B + GATE) % RING
                split_after(b, slot)
                act.wait_ge(block_done, b + 1)
                for t in range(TT):
                    nc.scalar.activation(gates[:, t, :, :].rearrange("p a b -> p (a b)"),
                                         bank[slot][:, 48 * t:48 * t + 48], ACT.Sigmoid,
                                         scale=rcol[:, t, 0:1]).then_inc(gate_ready, 1)
                act.wait_ge(vcb_zero, 2 * (a + 1))
                act.wait_ge(vcmp_hi, a + 1)
                for g in range(GROUPS):
                    for j in range(4):
                        nc.scalar.activation(sm_hi[32 * j:32 * j + 32, g, DH * j:DH * j + DH],
                                             f32(vc_hi[32 * g:32 * g + 32, :]), ACT.Copy).then_inc(vcb_hi, 1)
                for j in range(4):
                    split_after(B + V + j, (B + V + j) % RING)
                act.wait_ge(block_done, B + V + 4)
                for t in range(TT):
                    nc.scalar.activation(val_hi[:, t, :, 0:DH],
                                         bank[(B + V + t) % RING][:, :].rearrange("p (n c) -> p n c", c=DH),
                                         ACT.Copy, scale=rcol[:, t, 0:1]).then_inc(val_hi_ready, 1)
                attention(a)
                out_projection(l)

            def attention(a):
                def group(g):
                    u0 = g * 36
                    for j in range(4):
                        h = 64 * (j % 2)
                        wait_past(act, pv_done, u0 + 144 * a)
                        nc.scalar.activation(q_st[h:h + 64, j:j + 1, :], qf[h:h + 64, bass.ds(g * 2 + j // 2, 1), :],
                                             ACT.Copy, scale=DH ** -0.5).then_inc(q_hi_ready, 1)
                    for s in range(36 + 8):
                        if 0 <= s - 2 < 36:
                            k = s - 2
                            u = u0 + (144 * a + k)
                            width = P if k % 9 == 0 else P * (k // 9 + 1)
                            act.wait_ge(prob_t, u + 1)
                            if not (a == 0 and k < 2):
                                wait_past(act, pv_done, u - 1)
                            else:
                                wait_past(act, pv_done, u0)
                            nc.scalar.activation(pt_hi[:, k % 2, 0:width], bank[2 + k % 2][:, 0:width], ACT.Copy
                                                 ).then_inc(pt_hi_ready, 1)
                        if s < 36:
                            u = u0 + (144 * a + s)
                            width = P if s % 9 == 0 else P * (s // 9 + 1)
                            act.wait_ge(max_ready, u + 1)
                            if a == 0 and s < 3:
                                wait_past(act, prob_t, u0)
                            else:
                                wait_past(act, prob_t, u - 2)
                            if s % 9 == 0:
                                nc.scalar.activation(tmp[:, s % 3, 0:P], tmp[:, s % 3, 0:P], ACT.Exp
                                                     ).then_inc(prob_ready, 1)
                            else:
                                nc.scalar.activation(tmp[:, s % 3, 0:width], bank[s % 2][:, 0:width], ACT.Exp,
                                                     bias=nmax[:, s % 4, 0:1]).then_inc(prob_ready, 1)
                        if s % 9 == 7 and s >= 16:
                            t = (s - 16) // 9
                            e = g * TT + (16 * a + t)
                            act.wait_ge(ot_ready, e + 1)
                            nc.scalar.activation(
                                mix_hi[:, bass.ds(g * 2, 2), bass.ts(t, P)],
                                bank[7][:, 0:256].rearrange("p (j q) -> p j q", j=2), ACT.Copy
                            ).then_inc(ot_hi_ready, 1)

                if a == 0:
                    group(0)
                with act.Fori(1 if a == 0 else 0, GROUPS) as g:
                    group(g)

            def sgu(l):
                B = plan.mix[l]
                sum_split(norm_of_mixer(l))
                for half in range(2):
                    for j in range(4):
                        b = B + 4 * half + j
                        split_after(b, b % RING)
                        if half == 0 and j == 0:
                            root(norm_of_mixer(l))
                            act.dma_start(bs_t, b_s.partition_broadcast(P)).then_inc(bs_full, 16)
                            act.wait_ge(norm_step, 5 * (norm_of_mixer(l) + 1))
                    act.wait_ge(block_done, B + 4 * half + 4)
                    for t in range(TT):
                        nc.scalar.activation(sgu_v[:, t, bass.ts(half, S)], bank[(B + t) % RING][:, :],
                                             ACT.Gelu_apprx_tanh, scale=rcol[:, t, 0:1]).then_inc(v_gelu, 1)
                split_after(B + SGU_WS, (B + SGU_WS) % RING)
                act.wait_ge(ln_var, 1)
                nc.scalar.activation(lstd[:, 1, :], lstd[:, 0, :], ACT.Sqrt).then_inc(ln_std, 1)
                for t in range(TT):
                    act.wait_ge(vn_ready, t + 1)
                    nc.scalar.activation(v_hi[:, t, :], sgu_v[:, t, :], ACT.Copy).then_inc(vn_hi, 1)
                    if t < 3:
                        split_after(B + SGU_U + t, (B + SGU_U + t) % RING)
                for m in range(MT):
                    if m + 3 < MT:
                        split_after(B + SGU_U + m + 3, (B + SGU_U + m + 3) % RING)
                    act.wait_ge(taken, B + SGU_U + m + 1)
                    nc.scalar.activation(tmp[:, 1, :], tmp[:, 0, :], ACT.Gelu_apprx_tanh).then_inc(u_gelu, 1)
                    act.wait_ge(mix_full, m + 1)
                    nc.scalar.activation(mix_hi[:, m, :], tmp[:, 3, :], ACT.Copy).then_inc(mix_hi_ready, 1)
                out_projection(l)

            def pool(l):
                B = plan.mix[l]
                sum_split(norm_of_mixer(l))
                for m in range(MT):
                    split_after(B + m, (B + m) % RING)
                    if m == 0:
                        root(norm_of_mixer(l))
                    act.wait_ge(d_full, m + 1)
                    nc.scalar.activation(hid_hi[:, m, :], tmp[:, 3, :], ACT.Copy).then_inc(d_hi, 1)
                for i in range(2):
                    b = B + POOL_GRP + i
                    split_after(b, b % RING)
                    act.wait_ge(block_done, b + 1)
                    for q in range(4):
                        m = 4 * i + q
                        nc.scalar.activation(mix_hi[:, m, :], bank[q][:, :], ACT.Copy, scale=col("pool_scale", m)
                                             ).then_inc(y_hi, 1)
                out_projection(l)

            act.wait_ge(con_full, 16)
            nc.scalar.activation(ident[:, :], con[:, CON["ident"]:CON["ident"] + P], ACT.Copy).then_inc(con_ready, 1)
            nc.scalar.activation(tril[:, :], con[:, CON["tril"]:CON["tril"] + P], ACT.Copy).then_inc(con_ready, 1)
            nc.scalar.activation(swap[:, :], con[:, CON["swap"]:CON["swap"] + P], ACT.Copy).then_inc(con_ready, 1)
            nc.scalar.activation(ident_b[:, :], con[:, CON["ident"]:CON["ident"] + P], ACT.Copy
                                 ).then_inc(con_ready, 1)
            nc.scalar.activation(causal_b[:, :], con[:, CON["causal"]:CON["causal"] + P], ACT.Copy
                                 ).then_inc(con_ready, 1)
            nc.scalar.activation(cmask_b[:, :, :].rearrange("p a b -> p (a b)"),
                                 con[:, CON["cmask"]:CON["cmask"] + TT * P], ACT.Copy).then_inc(con_ready, 1)
            nc.scalar.activation(blk[:, :], con[:, CON["blk"]:CON["blk"] + 4], ACT.Copy).then_inc(con_ready, 1)
            act.wait_ge(par_full, 16)
            for m in range(MT):
                xs_high(0, m)
            for b in range(AHEAD):
                split(b)
            act.wait_ge(rope_step, ROPE_STEPS)
            nc.scalar.activation(rope[:, 1, :], tmp[:, 1, :], ACT.Sin).then_inc(rope_sin, 1)
            nc.scalar.activation(rope[:, 0, :], tmp[:, 2, :], ACT.Sin).then_inc(rope_sin, 1)
            a = 0
            for l, (kind, _) in enumerate(plan.mixers):
                if kind == "nsa":
                    nsa(l, a)
                    a += 1
                elif kind == "sgu":
                    sgu(l)
                else:
                    pool(l)
                ffn(l)
            sum_split(plan.norms - 1)
            root(plan.norms - 1)

        @block.vector
        def _(dve):
            def split(b, slot):
                k = slot % RAW
                dve.wait_ge(w_hi_ready, b + 1)
                nc.vector.tensor_tensor(w_lo[:, slot, :], raw[:, k, :], f32(w_hi[:, slot, :]), ALU.subtract
                                        ).then_inc(w_lo_ready, 1)

            def split_after(b, slot):
                split(b + AHEAD, (slot + AHEAD) % RING)

            def xs_low(n, m, at):
                dve.wait_ge(xs_hi_ready, at + 1)
                nc.vector.scalar_tensor_tensor(out=tile(xs_lo, m), in0=tile(x, m), scalar=g_of(n, m),
                                               in1=f32(tile(xh, m)), op0=ALU.mult, op1=ALU.subtract
                                               ).then_inc(xs_lo_ready, 1)

            def sum_split(n):
                dve.wait_ge(sq_hi_ready, n + 1)
                nc.vector.tensor_tensor(sq_lo, work[:, 0, :], f32(sq_hi), ALU.subtract).then_inc(sq_lo_ready, 1)

            def rsqrt_steps(v, y, t, sem_, base):
                nc.vector.reciprocal(y, y).then_inc(sem_, 1)
                dve.wait_ge(sem_, base + 1)
                nc.vector.tensor_tensor(t, y, y, ALU.mult).then_inc(sem_, 1)
                dve.wait_ge(sem_, base + 2)
                nc.vector.tensor_tensor(t, t, v, ALU.mult).then_inc(sem_, 1)
                dve.wait_ge(sem_, base + 3)
                nc.vector.tensor_scalar(t, t, -0.5, 1.5, ALU.mult, ALU.add).then_inc(sem_, 1)
                dve.wait_ge(sem_, base + 4)
                nc.vector.tensor_tensor(y, y, t, ALU.mult).then_inc(sem_, 1)
                dve.wait_ge(sem_, base + 5)

            def norm(n):
                dve.wait_ge(norm_sum, n + 1)
                nc.vector.tensor_scalar(vstat[:, 0:S], bank[4][:, :], 1.0 / D, RMS_EPS, ALU.mult, ALU.add
                                        ).then_inc(var_ready, 1)
                nc.vector.tensor_scalar(vstat[:, S:S + 2 * TT], bank[5][:, 0:2 * TT], 1.0 / D, RMS_EPS, ALU.mult,
                                        ALU.add).then_inc(var_ready, 1)
                dve.wait_ge(std_ready, n + 1)
                both = work[:, :, :].rearrange("p a b -> p (a b)")[:, 0:S + 2 * TT]
                rsqrt_steps(vstat[:, :], rstat[:, :], both, norm_step, 5 * n)

            def add_residual(m, b, slot):
                dve.wait_ge(block_done, b + 1)
                nc.vector.tensor_tensor(tile(x, m), bank[slot][:, :], tile(x, m), ALU.add).then_inc(taken, 1)

            def out_projection(l):
                n, b0 = norm_of_ffn(l), plan.out_block(l)
                s0 = b0 % RING
                with dve.Fori(0, MT // RING) as i:
                    for k in range(RING):
                        b, slot, m = i * RING + (b0 + k), (s0 + k) % RING, i * RING + k
                        split_after(b, slot)
                        add_residual(m, b, slot)
                        dve.wait_ge(taken, b + 1)
                        xs_low(n, m, m + MT * n)

            def ffn(l):
                n = norm_of_ffn(l)
                last = n + 1 == plan.norms - 1
                for p, tiles in enumerate(PARTS):
                    up, down = plan.part_block(l, p)
                    s0 = up % RING
                    t0 = HIDDEN_TILES * l + 8 * p

                    def pair(i):
                        for k in range(2):
                            t, b, slot = i * 2 + (t0 + k), i * 4 + (up + 2 * k), (s0 + 2 * k) % RING
                            split_after(b, slot)
                            if p == 0 and k == 0 and type(i) is int:
                                norm(n)
                            dve.wait_ge(block_done, b + 1)
                            nc.vector.tensor_tensor(tmp[:, 0, :], bank[slot][:, :], rrow, ALU.mult
                                                    ).then_inc(taken, 1)
                            split_after(b + 1, (slot + 1) % RING)
                            dve.wait_ge(block_done, b + 2)
                            nc.vector.tensor_tensor(tmp[:, 2, :], bank[(slot + 1) % RING][:, :], rrow, ALU.mult
                                                    ).then_inc(taken, 1)
                            dve.wait_ge(taken, b + 2)
                            dve.wait_ge(silu_ready, t + 1)
                            nc.vector.tensor_tensor(tmp[:, 3, :], tmp[:, 1, :], tmp[:, 2, :], ALU.mult
                                                    ).then_inc(hid_full, 1)
                            dve.wait_ge(hid_full, t + 1)
                            dve.wait_ge(hid_hi_ready, t + 1)
                            h = bass.ds(i * 2 + k, 1)
                            nc.vector.tensor_tensor(hid_lo[:, h, :], tmp[:, 3:4, :], f32(hid_hi[:, h, :]),
                                                    ALU.subtract).then_inc(hid_lo_ready, 1)

                    first = 0
                    if p == 0:
                        sum_split(n)
                        pair(0)
                        first = 1
                    with dve.Fori(first, tiles // 2) as i:
                        pair(i)
                    s0d = down % RING
                    with dve.Fori(0, MT // RING) as i:
                        for k in range(RING):
                            b, slot, m = i * RING + (down + k), (s0d + k) % RING, i * RING + k
                            split_after(b, slot)
                            dve.wait_ge(taken, b)
                            add_residual(m, b, slot)
                            if p == len(PARTS) - 1 and not last:
                                dve.wait_ge(taken, b + 1)
                                xs_low(n + 1, m, m + MT * (n + 1))

            def nsa(l, a):
                B = plan.mix[l]
                n = norm_of_mixer(l)

                def rope_low(b, slot, rho):
                    dve.wait_ge(rq_hi_ready, rho + 1)
                    nc.vector.tensor_tensor(sq_lo, bank[slot][:, :], f32(sq_hi), ALU.subtract
                                            ).then_inc(rq_lo_ready, 1)

                def rotate(b, slot, rho, dst):
                    nc.vector.tensor_tensor(tmp[:, 2, :], bank[slot][:, :], work[:, 0, :], ALU.mult
                                            ).then_inc(taken, 1)
                    dve.wait_ge(swapped, rho + 1)
                    nc.vector.tensor_tensor(work2[:, 1, :], bank[5][:, :], work[:, 1, :], ALU.mult
                                            ).then_inc(rot_b, 1)
                    dve.wait_ge(taken, b + 1)
                    dve.wait_ge(rot_b, rho + 1)
                    nc.vector.tensor_tensor(dst, tmp[:, 2, :], work2[:, 1, :], ALU.add).then_inc(rotated, 1)

                def finish(j):
                    b, slot = B + j, (B + j) % RING
                    rt = tmp[:, j % 2, :]
                    if j == 2:
                        dve.wait_ge(kc_rows, 16 * a + 4)
                    if j == 3:
                        dve.wait_ge(kc_rows, 16 * a + 8)
                    if j in (4, 5):
                        dve.wait_ge(kc_rows, 16 * a + 4 * (j - 1))
                    if j in (6, 7):
                        dve.wait_ge(key_hi_ready, 16 * a + 4 * (j - 5))
                    if j in (VC, VC + 1):
                        dve.wait_ge(block_done, b + 1)
                        nc.vector.tensor_tensor(rt, bank[slot][:, :], rrow, ALU.mult).then_inc(taken, 1)
                        return
                    rho = 14 * a + (j if j < 2 else j - 2)
                    if rho:
                        dve.wait_ge(rotated, rho)
                    rotate(b, slot, rho, rt)
                    if j >= KS:
                        r = (j - KS) // 2
                        dve.wait_ge(rotated, rho + 1)
                        for half in range(2):
                            g = 2 * (j % 2) + half
                            src = rt[64 * half:64 * half + 64, :]
                            dve.wait_ge(key_hi_ready, 16 * a + 4 * (j - 4) + 2 * half + 1)
                            for h in (half, 1 - half):
                                nc.vector.tensor_tensor(key_lo[64 * h:64 * h + 64, r, g, :], src,
                                                        f32(key_hi[64 * half:64 * half + 64, r, g, :]),
                                                        ALU.subtract).then_inc(key_lo_ready, 1)

                def cm(c):
                    v, k0 = c // 4, 4 * (c % 4)
                    dve.wait_ge(kc_rows, 16 * a + 8 * (v + 1))
                    rows = bass.AP(tensor=big, offset=v * GROUPS * KCW + 2 * k0,
                                   ap=[[2 * GROUPS * KCW, P], [2, 4], [KCW, GROUPS], [16, NCMP]])
                    at = PAR["pos"] + 32 * l_nsa + 16 * v + k0
                    bias = bass.AP(tensor=par, offset=at, ap=[[PAR_COLS, P], [1, 4], [0, GROUPS], [0, NCMP]])
                    dst = tmp[:, 3, :].rearrange("p (k g n) -> p k g n", k=4, g=GROUPS)
                    if 8 * a + c:
                        dve.wait_ge(cm_lo_ready, 8 * a + c)
                    nc.vector.tensor_tensor(dst, rows, bias, ALU.add).then_inc(cm_full, 1)
                    dve.wait_ge(cm_full, 8 * a + c + 1)
                    dve.wait_ge(cm_hi_ready, 8 * a + c + 1)
                    nc.vector.tensor_tensor(cm_lo[:, v, bass.ts(c % 4, S)], tmp[:, 3, :],
                                            f32(cm_hi[:, v, bass.ts(c % 4, S)]), ALU.subtract
                                            ).then_inc(cm_lo_ready, 1)

                l_nsa = plan.mixers[l][1]
                sum_split(n)
                for v in range(2):
                    nc.vector.memset(kc2[:, v, :, S - 1:KCW], 0.0).then_inc(kc_pad, 1)
                for j in range(W1K):
                    b, slot = B + j, (B + j) % RING
                    split_after(b, slot)
                    if j == 0:
                        norm(n)
                        dve.wait_ge(rope_sin, 2)
                        for i in range(2):
                            nc.vector.tensor_tensor(work[:, i, :], rope[:, i, :], rrow, ALU.mult
                                                    ).then_inc(tab_ready, 1)
                        dve.wait_ge(tab_ready, 2 * (a + 1))
                    if j not in (VC, VC + 1):
                        rope_low(b, slot, 14 * a + (j if j < 2 else j - 2))
                    if j:
                        finish(j - 1)
                    if j >= 4:
                        cm(j - 4)
                finish(W1K - 1)
                for j in range(W1K, W2):
                    b, slot = B + j, (B + j) % RING
                    split_after(b, slot)
                    if j < W1K + 4:
                        cm(j - W1K + 4)
                    if j % 2:
                        q = (j - W1K) // 2
                        dve.wait_ge(ch_hi_ready, 4 * a + q + 1)
                        nc.vector.tensor_tensor(ch_lo[:, q, :], tmp[:, 2, bass.ts(q, P)], f32(ch_hi[:, q, :]),
                                                ALU.subtract).then_inc(taken, 2)
                b, slot = B + W2, (B + W2) % RING
                split_after(b, slot)
                dve.wait_ge(kcmp_hi, a + 1)
                dve.wait_ge(vcmp_hi, a + 1)
                nc.vector.tensor_tensor(vc_lo[:, :], vc_f, f32(vc_hi[:, :]), ALU.subtract
                                        ).then_inc(vcmp_lo, 1)
                nc.vector.tensor_tensor(kc_lo[:, :], bank[slot][:, 0:P], f32(kc_hi[:, :]), ALU.subtract
                                        ).then_inc(taken, 1)
                with dve.Fori(0, 2) as i:
                    for k in range(RING):
                        slot = (B + Q + k) % RING
                        b, rho = i * RING + (B + Q + k), i * RING + (14 * a + 6 + k)
                        split_after(b, slot)
                        rope_low(b, slot, rho)
                        if k:
                            dve.wait_ge(rotated, rho - 1)
                            rotate(b - 1, (slot - 1) % RING, rho - 1, tile(qf, i * RING + (k - 1)))
                    dve.wait_ge(rotated, rho)
                    rotate(b, slot, rho, tile(qf, i * RING + (RING - 1)))
                b, slot = B + GATE, (B + GATE) % RING
                split_after(b, slot)
                dve.wait_ge(gate_ready, 4 * (a + 1))
                nc.vector.tensor_scalar(gates[:, 0, 0, :], gates[:, 0, 0, :], col("anyvalid", 0), None, ALU.mult
                                        ).then_inc(taken, 1)
                dve.wait_ge(vcb_zero, 2 * (a + 1))
                dve.wait_ge(vcmp_lo, a + 1)
                for g in range(GROUPS):
                    for j in range(4):
                        nc.vector.tensor_copy(sm_lo[32 * j:32 * j + 32, g, DH * j:DH * j + DH],
                                              f32(vc_lo[32 * g:32 * g + 32, :])).then_inc(vcb_lo, 1)
                for j in range(4):
                    split_after(B + V + j, (B + V + j) % RING)
                dve.wait_ge(block_done, B + V + 4)
                nc.vector.memset(f32(val_hi[:, :, :, DH:DH + 1]), 1.0).then_inc(val_ones, 1)
                nc.vector.memset(f32(val_hi[:, :, :, DH + 1:DH + 2]), 0.0).then_inc(val_ones, 1)
                for t in range(TT):
                    dve.wait_ge(val_hi_ready, 4 * a + t + 1)
                    psum = bank[(B + V + t) % RING][:, :].rearrange("p (n c) -> p n c", c=DH)
                    nc.vector.scalar_tensor_tensor(out=val_lo[:, t, :, :], in0=psum, scalar=rcol[:, t, 0:1],
                                                   in1=f32(val_hi[:, t, :, 0:DH]), op0=ALU.mult,
                                                   op1=ALU.subtract).then_inc(taken, 1)
                attention(a)
                out_projection(l)

            def attention(a):
                def group(g):
                    u0 = g * 36
                    for j in range(4):
                        h = 64 * (j % 2)
                        dve.wait_ge(q_hi_ready, g * 4 + (16 * a + j + 1))
                        nc.vector.scalar_tensor_tensor(
                            out=q_st[64 - h:128 - h, j:j + 1, :], in0=qf[h:h + 64, bass.ds(g * 2 + j // 2, 1), :],
                            scalar=DH ** -0.5, in1=f32(q_st[h:h + 64, j:j + 1, :]), op0=ALU.mult, op1=ALU.subtract
                        ).then_inc(q_lo_ready, 1)
                    for s in range(36 + 8):
                        if s < 36:
                            u = u0 + (144 * a + s)
                            width = P if s % 9 == 0 else P * (s // 9 + 1)
                            dve.wait_ge(score_ready, u + 1)
                            if s % 9 == 0:
                                sc = bank[s % 2][:, 0:P].rearrange("p (j n) -> p j n", j=4)
                                e = g * TT + (16 * a + s // 9)
                                nc.vector.tensor_reduce(nmax[:, s % 4, :], sc, AX.X, ALU.max, negate=True
                                                        ).then_inc(cmax_ready, 1)
                                dve.wait_ge(cmax_ready, e + 1)
                                if a == 0 and s < 3:
                                    wait_past(dve, prob_t, u0)
                                else:
                                    wait_past(dve, prob_t, u - 2)
                                nc.vector.tensor_tensor(
                                    tmp[:, s % 3, 0:P].rearrange("p (j n) -> p j n", j=4), sc,
                                    nmax[:, s % 4, :].unsqueeze(2).broadcast_to([P, 4, NCMP]), ALU.add
                                ).then_inc(max_ready, 1)
                            else:
                                nc.vector.tensor_reduce(nmax[:, s % 4, 0:1], bank[s % 2][:, 0:width], AX.X,
                                                        ALU.max, negate=True).then_inc(max_ready, 1)
                        if 0 <= s - 2 < 36:
                            k = s - 2
                            u = u0 + (144 * a + k)
                            width = P if k % 9 == 0 else P * (k // 9 + 1)
                            dve.wait_ge(pt_hi_ready, u + 1)
                            nc.vector.tensor_tensor(pt_lo[:, k % 2, 0:width], bank[2 + k % 2][:, 0:width],
                                                    f32(pt_hi[:, k % 2, 0:width]), ALU.subtract
                                                    ).then_inc(pt_lo_ready, 1)
                        if s >= 12 and (s - 12) % 9 == 0:
                            evacuate(a, g, (s - 12) // 9)
                        if s % 9 == 7 and s >= 16:
                            t = (s - 16) // 9
                            e = g * TT + (16 * a + t)
                            dve.wait_ge(ot_hi_ready, e + 1)
                            nc.vector.tensor_tensor(
                                mix_lo[:, bass.ds(g * 2, 2), bass.ts(t, P)],
                                bank[7][:, 0:256].rearrange("p (j q) -> p j q", j=2),
                                f32(mix_hi[:, bass.ds(g * 2, 2), bass.ts(t, P)]), ALU.subtract
                            ).then_inc(ot_lo_ready, 1)

                if a == 0:
                    group(0)
                with dve.Fori(1 if a == 0 else 0, GROUPS) as g:
                    group(g)

            def evacuate(a, g, t):
                e = g * TT + (16 * a + t)
                dve.wait_ge(pv_done, g * 36 + (144 * a + 9 * (t + 1)))
                heads = [bank[4 + r][:, 0:4 * VW].rearrange("p (j c) -> p j c", c=VW) for r in range(2)]
                nc.vector.reciprocal(den[:, 0, :], bank[6][:, 256:260]).then_inc(den_step, 1)
                nc.vector.reciprocal(den[:, 1, :], heads[0][:, :, DH]).then_inc(den_step, 1)
                nc.vector.reciprocal(den[:, 2, :], heads[1][:, :, DH]).then_inc(den_step, 1)
                dve.wait_ge(den_step, e * 4 + 3)
                nc.vector.tensor_tensor(wgt[:, :, :], den[:, :, :], gates[:, t, :, bass.ds(g * 4, 4)], ALU.mult
                                        ).then_inc(den_step, 1)
                dve.wait_ge(den_step, e * 4 + 4)
                wait_past(dve, o_full, e)
                wide = [wgt[:, r, :].unsqueeze(2).broadcast_to([P, 4, DH]) for r in range(3)]
                terms = [work[:, 1, 0:256], work[:, 0, 0:256], work[:, 0, 256:512]]
                for r in (1, 2):
                    nc.vector.tensor_tensor(terms[r].rearrange("p (j c) -> p j c", c=DH), heads[r - 1][:, :, 0:DH],
                                            wide[r], ALU.mult).then_inc(o_step, 1)
                nc.vector.tensor_tensor(terms[0].rearrange("p (j c) -> p j c", c=DH),
                                        bank[6][:, 0:256].rearrange("p (j c) -> p j c", c=DH), wide[0], ALU.mult
                                        ).then_inc(o_step, 1)

            def sgu(l):
                B = plan.mix[l]
                sum_split(norm_of_mixer(l))
                for half in range(2):
                    for j in range(4):
                        b = B + 4 * half + j
                        split_after(b, b % RING)
                        if half == 0 and j == 0:
                            norm(norm_of_mixer(l))
                    if half:
                        slot = (B + SGU_WS) % RING
                        low = tril[:, :].unsqueeze(1).broadcast_to([P, 8, P])
                        dve.wait_ge(w_lo_ready, B + SGU_WS + 1)
                        for dst, src in ((ws_hi, w_hi), (ws_lo, w_lo)):
                            nc.vector.tensor_tensor(
                                dst.rearrange("p (g t) -> p g t", g=8),
                                f32(src[:, slot, :]).rearrange("p (g t) -> p g t", g=8), low, ALU.mult
                            ).then_inc(ws_masked, 1)
                    for t in range(TT):
                        dve.wait_ge(v_gelu, 4 * half + t + 1)
                        nc.vector.bn_stats(bnst[:, t, half, :], sgu_v[:, t, bass.ts(half, S)]).then_inc(taken, 1)
                split_after(B + SGU_WS, (B + SGU_WS) % RING)
                dve.wait_ge(taken, B + 8)
                for t in range(TT):
                    nc.vector.bn_aggr(mv[:, t, :], bnst[:, t, :, :].rearrange("p a b -> p (a b)")).then_inc(ln_step, 1)
                dve.wait_ge(ln_step, TT)
                nc.vector.tensor_scalar(lstd[:, 0, :], mv[:, :, 1], LN_EPS, None, ALU.add).then_inc(ln_var, 1)
                dve.wait_ge(ln_std, 1)
                rsqrt_steps(lstd[:, 0, :], lstd[:, 1, :], lstd[:, 2, :], ln_step, TT)
                for t in range(TT):
                    nc.vector.tensor_scalar(sgu_v[:, t, :], sgu_v[:, t, :], mv[:, t, 0:1], lstd[:, 1, t:t + 1],
                                            ALU.subtract, ALU.mult).then_inc(vn_ready, 1)
                    dve.wait_ge(vn_hi, t + 1)
                    nc.vector.tensor_tensor(v_lo[:, t, :], sgu_v[:, t, :], f32(v_hi[:, t, :]), ALU.subtract
                                            ).then_inc(vn_lo, 1)
                    if t < 3:
                        split_after(B + SGU_U + t, (B + SGU_U + t) % RING)
                dve.wait_ge(block_done, B + SGU_WS + 1)
                dve.wait_ge(bs_full, 16)
                for g in range(8):
                    nc.vector.scalar_tensor_tensor(
                        out=bias_t[:, bass.ts(g, P)], in0=bank[4 + g // 4][:, bass.ts(g % 4, P)],
                        scalar=col("ln_b", g), in1=bs_t[:, bass.ts(g, P)], op0=ALU.mult, op1=ALU.add
                    ).then_inc(bias_ready if g < 7 else taken, 1)
                for m in range(MT):
                    b = B + SGU_U + m
                    if m + 3 < MT:
                        split_after(b + 3, (b + 3) % RING)
                    dve.wait_ge(block_done, b + 1)
                    nc.vector.tensor_tensor(tmp[:, 0, :], bank[b % RING][:, :], rrow, ALU.mult).then_inc(taken, 1)
                    dve.wait_ge(mixed, m + 1)
                    dve.wait_ge(taken, B + SGU_U)
                    nc.vector.scalar_tensor_tensor(
                        out=tmp[:, 2, :].rearrange("p (n t) -> p n t", n=TT),
                        in0=bank[6 + m % 2][:, :].rearrange("p (n t) -> p n t", n=TT), scalar=col("ln_g", m),
                        in1=bias_t[:, bass.ts(m, P)].unsqueeze(1).broadcast_to([P, TT, P]),
                        op0=ALU.mult, op1=ALU.add).then_inc(sv_ready, 1)
                    dve.wait_ge(sv_ready, m + 1)
                    dve.wait_ge(u_gelu, m + 1)
                    nc.vector.tensor_tensor(tmp[:, 3, :], tmp[:, 1, :], tmp[:, 2, :], ALU.mult).then_inc(mix_full, 1)
                    dve.wait_ge(mix_full, m + 1)
                    dve.wait_ge(mix_hi_ready, m + 1)
                    nc.vector.tensor_tensor(mix_lo[:, m, :], tmp[:, 3, :], f32(mix_hi[:, m, :]), ALU.subtract
                                            ).then_inc(mix_lo_ready, 1)
                out_projection(l)

            def pool(l):
                B = plan.mix[l]
                width = POOL_PAD + S
                bufs = [big[:, i * width:(i + 1) * width] for i in range(3)]
                sum_split(norm_of_mixer(l))
                for z in bufs:
                    nc.vector.memset(z[:, 0:POOL_PAD], 0.0).then_inc(z_pad, 1)
                steps = 0
                for m in range(MT):
                    b = B + m
                    split_after(b, b % RING)
                    if m == 0:
                        norm(norm_of_mixer(l))
                        dve.wait_ge(z_pad, 3)
                    gi = m // 2
                    dve.wait_ge(block_done, b + 1)
                    nc.vector.tensor_tensor(bufs[0][:, POOL_PAD:], bank[b % RING][:, :], rrow, ALU.mult
                                            ).then_inc(taken, 1)
                    dve.wait_ge(taken, b + 1)
                    cur = bufs[0]
                    for s in range(gi + 1):
                        nxt = bufs[1 + s % 2]
                        nc.vector.tensor_tensor(nxt[:, POOL_PAD:], cur[:, POOL_PAD:],
                                                cur[:, POOL_PAD - 2 ** s:width - 2 ** s], ALU.add
                                                ).then_inc(pool_step, 1)
                        steps += 1
                        dve.wait_ge(pool_step, steps)
                        cur = nxt
                    head = cur[:, POOL_PAD:2 * POOL_PAD]
                    at = PAR["corr"] + gi * POOL_PAD
                    nc.vector.tensor_tensor(head, head, par[:, at:at + POOL_PAD], ALU.mult).then_inc(pool_step, 1)
                    steps += 1
                    dve.wait_ge(pool_step, steps)
                    nc.vector.scalar_tensor_tensor(out=tmp[:, 3, :], in0=cur[:, POOL_PAD:], scalar=0.5 ** (gi + 1),
                                                   in1=bufs[0][:, POOL_PAD:], op0=ALU.mult, op1=ALU.subtract
                                                   ).then_inc(d_full, 1)
                    dve.wait_ge(d_full, m + 1)
                    dve.wait_ge(d_hi, m + 1)
                    nc.vector.tensor_tensor(hid_lo[:, m, :], tmp[:, 3, :], f32(hid_hi[:, m, :]), ALU.subtract
                                            ).then_inc(d_lo, 1)
                for i in range(2):
                    b = B + POOL_GRP + i
                    split_after(b, b % RING)
                    for q in range(4):
                        m = 4 * i + q
                        dve.wait_ge(y_hi, m + 1)
                        nc.vector.scalar_tensor_tensor(
                            out=mix_lo[:, m, :], in0=bank[q][:, :], scalar=col("pool_scale", m),
                            in1=f32(mix_hi[:, m, :]), op0=ALU.mult, op1=ALU.subtract
                        ).then_inc(y_lo if q < 3 else taken, 1)
                out_projection(l)

            nc.vector.memset(f32(ones[:, :]), 1.0).then_inc(ones_ready, 1)
            dve.wait_ge(par_full, 16)
            for m in range(MT):
                xs_low(0, m, m)
            for b in range(AHEAD):
                split(b, b)
            dve.wait_ge(pos_full, 16)
            ang, turn, aux = tmp[:, 3, :], tmp[:, 2, :], tmp[:, 0, :]
            def angle_step(i, ins):
                ins.then_inc(rope_step, 1)
                dve.wait_ge(rope_step, i)

            angle_step(1, nc.vector.tensor_copy(ang, tmp[:, 0, :].bitcast(I32)))
            angle_step(2, nc.vector.tensor_scalar(ang, ang, col("invf", 0), None, ALU.mult))
            angle_step(3, nc.vector.tensor_scalar(turn, ang, float(0.5 / np.pi), None, ALU.mult))
            angle_step(4, nc.vector.tensor_scalar(turn, turn, ROUND, None, ALU.add))
            angle_step(5, nc.vector.tensor_scalar(turn, turn, -ROUND, None, ALU.add))
            for i in range(3):
                angle_step(6 + i, nc.vector.scalar_tensor_tensor(out=ang, in0=turn, scalar=-TWO_PI[i], in1=ang,
                                                                 op0=ALU.mult, op1=ALU.add))
            angle_step(9, nc.vector.tensor_scalar(tmp[:, 1, :], ang, PI_F, -PI_F, ALU.min, ALU.max))
            angle_step(10, nc.vector.tensor_scalar(turn, ang, float(np.pi / 2), None, ALU.add))
            angle_step(11, nc.vector.tensor_scalar(aux, turn, float(np.pi), -2.0 * float(np.pi), ALU.is_gt,
                                                   ALU.mult))
            angle_step(12, nc.vector.tensor_tensor(turn, turn, aux, ALU.add))
            angle_step(13, nc.vector.tensor_scalar(turn, turn, PI_F, -PI_F, ALU.min, ALU.max))
            dve.wait_ge(con_ready, 7)
            dve.wait_ge(rope_sin, 2)
            a = 0
            for l, (kind, _) in enumerate(plan.mixers):
                if kind == "nsa":
                    nsa(l, a)
                    a += 1
                elif kind == "sgu":
                    sgu(l)
                else:
                    pool(l)
                ffn(l)
            n = plan.norms - 1
            sum_split(n)
            norm(n)
            for m in range(MT):
                nc.vector.scalar_tensor_tensor(out=qf[:, m, :], in0=x[:, m, :], scalar=g_of(n, m), in1=rrow,
                                               op0=ALU.mult, op1=ALU.mult).then_inc(y_out, 1)

        @block.tensor
        def _(pe):
            def mm(out_, w, v, start, stop):
                return nc.tensor.matmul(out_, w, v, start=start, stop=stop)

            def mm3(out_, w, v, start, stop):
                mm(out_, w[0], v[0], start, False)
                mm(out_, w[0], v[1], False, False)
                return mm(out_, w[1], v[0], False, stop)

            def wslot(slot, at, n=P):
                return w_hi[:, slot, at:at + n], w_lo[:, slot, at:at + n]

            def open_block(b):
                pe.wait_ge(w_lo_ready, b + 1)
                if not (type(b) is int and b < RING):
                    pe.wait_ge(taken, b - RING + 1)

            def project(b, slot, nk, mov, ready=None):
                open_block(b)
                for k in range(nk):
                    if ready is not None:
                        pe.wait_ge(ready[0], ready[1] + k + 1)
                    last = mm3(bank[slot][:, :], wslot(slot, k * P), mov(k), k == 0, k == nk - 1)
                last.then_inc(block_done, 1)

            xs = lambda k: (xh[:, k, :], xs_lo[:, k, :])
            hid = lambda k: (hid_hi[:, k, :], hid_lo[:, k, :])
            mix = lambda k: (mix_hi[:, k, :], mix_lo[:, k, :])

            def norm(n):
                pe.wait_ge(sq_lo_ready, n + 1)
                if n == 0:
                    pe.wait_ge(ones_ready, 1)
                mm(bank[4][:, :], ones[:, :], sq_hi, True, False)
                mm(bank[4][:, :], ones[:, :], sq_lo, False, True)
                for t in range(TT):
                    mm(bank[5][:, 2 * t:2 * t + 2], sq_hi[:, bass.ts(t, P)], ones[:, 0:2], True, False)
                    last = mm(bank[5][:, 2 * t:2 * t + 2], sq_lo[:, bass.ts(t, P)], ones[:, 0:2], False, True)
                last.then_inc(norm_sum, 1)

            def out_projection(l, ready=None):
                b0 = plan.out_block(l)
                s0 = b0 % RING
                with pe.Fori(0, MT // RING) as i:
                    for k in range(RING):
                        project(i * RING + (b0 + k), (s0 + k) % RING, MT, mix, ready if k == 0 else None)

            def ffn(l):
                n = norm_of_ffn(l)
                for p, tiles in enumerate(PARTS):
                    up, down = plan.part_block(l, p)
                    s0 = up % RING
                    t0 = HIDDEN_TILES * l + 8 * p
                    first = 0
                    if p == 0:
                        project(up, s0, MT, xs, (xs_lo_ready, MT * n))
                        norm(n)
                        for k in range(1, RING):
                            project(up + k, (s0 + k) % RING, MT, xs)
                        first = 1
                    with pe.Fori(first, tiles // 2) as i:
                        for k in range(RING):
                            project(i * RING + (up + k), (s0 + k) % RING, MT, xs)
                    s0d = down % RING
                    with pe.Fori(0, MT // RING) as i:
                        for k in range(RING):
                            project(i * RING + (down + k), (s0d + k) % RING, tiles, hid,
                                    (hid_lo_ready, t0) if k == 0 else None)

            def swap_rows(rho):
                pe.wait_ge(rq_lo_ready, rho + 1)
                if not (type(rho) is int and rho == 0):
                    pe.wait_ge(rot_b, rho)
                mm(bank[5][:, :], swap[:, :], sq_hi, True, False)
                mm(bank[5][:, :], swap[:, :], sq_lo, False, True).then_inc(swapped, 1)

            def values(b0, banks, free, width=S):
                pe.wait_ge(taken, free)
                for j in range(4):
                    pe.wait_ge(w_lo_ready, b0 + j + 1)
                    for kk in range(2):
                        k = 2 * j + kk
                        for t in range(TT):
                            x_t = (xh[:, k, bass.ts(t, P)], xs_lo[:, k, bass.ts(t, P)])
                            last = mm3(bank[banks[t]][:, :], x_t, wslot((b0 + j) % RING, kk * S, S), k == 0, k == 7)
                    last.then_inc(block_done, 1)

            def nsa(l, a):
                B = plan.mix[l]
                n = norm_of_mixer(l)
                for j in range(W1K):
                    project(B + j, (B + j) % RING, MT, xs, (xs_lo_ready, MT * n) if j == 0 else None)
                    if j == 0:
                        norm(n)
                    if j and j - 1 not in (VC, VC + 1):
                        swap_rows(14 * a + (j - 1 if j - 1 < 2 else j - 3))
                swap_rows(14 * a + 5)
                for j in range(W1K, W2):
                    b, slot = B + j, (B + j) % RING
                    v, half = (j - W1K) // 4, j % 2
                    open_block(b)
                    dst = bank[slot if not half else (slot - 1) % RING][:, 0:P]
                    for k in range(8):
                        kt = 8 * half + k
                        if kt % 4 == 0:
                            pe.wait_ge(cm_lo_ready, 8 * a + 4 * v + kt // 4 + 1)
                        last = mm3(dst, wslot(slot, k * P), (cm_hi[:, v, bass.ts(kt, P)], cm_lo[:, v, bass.ts(kt, P)]),
                                   kt == 0, kt == 15)
                    last.then_inc(block_done, 1)
                b, slot = B + W2, (B + W2) % RING
                open_block(b)
                pe.wait_ge(taken, b)
                for q in range(2):
                    mm3(bank[slot][:, 0:P], wslot(slot, q * P), (ch_hi[:, q, :], ch_lo[:, q, :]), q == 0, q == 1)
                for q in range(2):
                    last = mm3(bank[6][:, 0:DH], (ch_hi[:, 2 + q, :], ch_lo[:, 2 + q, :]),
                               wslot(slot, 2 * P + q * DH, DH), q == 0, q == 1)
                last.then_inc(block_done, 1)
                with pe.Fori(0, 2) as i:
                    for k in range(RING):
                        project(i * RING + (B + Q + k), (B + Q + k) % RING, MT, xs)
                        if k:
                            swap_rows(i * RING + (14 * a + 6 + k - 1))
                    swap_rows(i * RING + (14 * a + 6 + RING - 1))
                b, slot = B + GATE, (B + GATE) % RING
                open_block(b)
                for t in range(TT):
                    for k in range(MT):
                        last = mm3(bank[slot][:, 48 * t:48 * t + 48], (xh[:, k, bass.ts(t, P)], xs_lo[:, k, bass.ts(t, P)]),
                                   wslot(slot, k * 48, 48), k == 0, k == MT - 1)
                last.then_inc(block_done, 1)
                values(B + V, [(B + V + t) % RING for t in range(TT)], B + V)
                attention(l, a)
                out_projection(l)

            def attention(l, a):
                pe.wait_ge(taken, plan.mix[l] + NSA_OUT)
                pe.wait_ge(val_ones, 2 * (a + 1))
                pe.wait_ge(key_hi_ready, 16 * (a + 1))
                pe.wait_ge(key_lo_ready, 16 * (a + 1))
                pe.wait_ge(vcb_hi, 16 * (a + 1))
                pe.wait_ge(vcb_lo, 16 * (a + 1))
                pe.wait_ge(con_ready, 7)

                def scores(g, s):
                    t, r = s // 9, s % 9
                    dst = bank[s % 2]
                    u = g * 36 + (144 * a + s)
                    if a == 0 and s < 2:
                        wait_past(pe, prob_ready, g * 36)
                    else:
                        wait_past(pe, prob_ready, u - 1)
                    if s == 0:
                        pe.wait_ge(q_lo_ready, g * 4 + (16 * a + 4))
                    if r == 0:
                        mm(dst[:, 0:P], ident_b[:, :], cmask_b[:, t, :], True, False)
                        for j in range(4):
                            q = q_st[:, j, bass.ts(t, P)]
                            mm(dst[:, bass.ts(j, NCMP)], q, kc_hi[:, bass.ds(g * NCMP, NCMP)], False, False)
                            last = mm(dst[:, bass.ts(j, NCMP)], q, kc_lo[:, bass.ds(g * NCMP, NCMP)], False, j == 3)
                    else:
                        br, j = (r - 1) // 4, (r - 1) % 4
                        q = q_st[:, j, bass.ts(t, P)]
                        width = P * (t + 1)
                        keys = [k[:, br, bass.ds(g, 1), 0:width].rearrange("p o t -> p (o t)")
                                for k in (key_hi, key_lo)]
                        mm(dst[:, 0:width], q, keys[0], True, False)
                        mm(dst[:, 0:width], q, keys[1], False, False)
                        last = mm(dst[:, bass.ts(t, P)], ident_b[:, :], causal_b[:, :], False, True)
                    last.then_inc(score_ready, 1)

                def turn(g, s):
                    u = g * 36 + (144 * a + s)
                    pe.wait_ge(prob_ready, u + 1)
                    if a == 0 and s < 2:
                        wait_past(pe, pt_lo_ready, g * 36)
                    else:
                        wait_past(pe, pt_lo_ready, u - 1)
                    for kb in range(1 if s % 9 == 0 else s // 9 + 1):
                        last = nc.tensor.transpose(bank[2 + s % 2][:, bass.ts(kb, P)],
                                                   tmp[:, s % 3, bass.ts(kb, P)], ident[:, :])
                    last.then_inc(prob_t, 1)

                def products(g, s):
                    t, r = s // 9, s % 9
                    pe.wait_ge(pt_lo_ready, g * 36 + (144 * a + s + 1))
                    if r == 0:
                        wait_past(pe, o_step, g * 12 + (48 * a + 3 * t))
                        p = (pt_hi[:, s % 2, 0:P], pt_lo[:, s % 2, 0:P])
                        v = [m[:, bass.ds(g, 1), :].rearrange("p o c -> p (o c)") for m in (sm_hi, sm_lo)]
                        mm3(bank[6][:, 0:256], p, v, True, True)
                        mm(bank[6][:, 256:260], p[0], blk[:, :], True, False)
                        last = mm(bank[6][:, 256:260], p[1], blk[:, :], False, True)
                    else:
                        br, j = (r - 1) // 4, (r - 1) % 4
                        o = bank[4 + br][:, j * VW:(j + 1) * VW]
                        for kb in range(t + 1):
                            vh, vl = [v[:, kb, bass.ds(g + 4 * br, 1), :].rearrange("p o c -> p (o c)")
                                      for v in (val_hi, val_lo)]
                            mm(o, pt_hi[:, s % 2, bass.ts(kb, P)], vh, kb == 0, False)
                            mm(o[:, 0:DH], pt_hi[:, s % 2, bass.ts(kb, P)], vl, False, False)
                            last = mm(o, pt_lo[:, s % 2, bass.ts(kb, P)], vh, False, kb == t)
                    last.then_inc(pv_done, 1)

                def group(g):
                    for s in range(36 + 8):
                        if s < 36:
                            scores(g, s)
                        if 0 <= s - 2 < 36:
                            turn(g, s - 2)
                        if 0 <= s - 3 < 36:
                            products(g, s - 3)
                        if s >= 15 and (s - 15) % 9 == 0:
                            e = g * TT + (16 * a + (s - 15) // 9)
                            pe.wait_ge(o_full, e + 1)
                            wait_past(pe, ot_lo_ready, e)
                            for j in range(2):
                                last = nc.tensor.transpose(bank[7][:, bass.ts(j, P)], work2[:, 0, bass.ts(j, P)],
                                                           ident[:, :])
                            last.then_inc(ot_ready, 1)

                if a == 0:
                    group(0)
                with pe.Fori(1 if a == 0 else 0, GROUPS) as g:
                    group(g)
                pe.wait_ge(ot_lo_ready, 16 * (a + 1))

            def sgu(l):
                B = plan.mix[l]
                n = norm_of_mixer(l)
                for k in range(MT):
                    pe.wait_ge(xs_lo_ready, MT * n + k + 1)
                norm(n)
                for half in range(2):
                    values(B + 4 * half, [(B + t) % RING for t in range(TT)], B + 4 * half)
                b = B + SGU_WS
                pe.wait_ge(ws_masked, 2)
                for h in range(2):
                    mm(bank[4 + h][:, :], ones[:, :], ws_hi[:, bass.ts(h, S)], True, False)
                    last = mm(bank[4 + h][:, :], ones[:, :], ws_lo[:, bass.ts(h, S)], False, True)
                last.then_inc(block_done, 1)
                for m in range(MT + 3):
                    if m >= 3:
                        q = m - 3
                        if q == 0:
                            pe.wait_ge(vn_lo, TT)
                        if q >= 2:
                            pe.wait_ge(sv_ready, q - 1)
                        for t in range(TT):
                            last = mm3(bank[6 + q % 2][:, bass.ts(t, P)],
                                       (v_hi[:, t, bass.ts(q, P)], v_lo[:, t, bass.ts(q, P)]),
                                       (ws_hi[:, bass.ts(q, P)], ws_lo[:, bass.ts(q, P)]), True, True)
                        last.then_inc(mixed, 1)
                    if m < MT:
                        project(B + SGU_U + m, (B + SGU_U + m) % RING, MT, xs)
                out_projection(l, (mix_lo_ready, 0))

            def pool(l):
                B = plan.mix[l]
                n = norm_of_mixer(l)
                for m in range(MT):
                    project(B + m, (B + m) % RING, MT, xs, (xs_lo_ready, MT * n) if m == 0 else None)
                    if m == 0:
                        norm(n)
                for i in range(2):
                    b = B + POOL_GRP + i
                    slot = b % RING
                    pe.wait_ge(w_lo_ready, b + 1)
                    if i == 0:
                        pe.wait_ge(taken, b)
                    for q in range(4):
                        if i:
                            if q < 3:
                                pe.wait_ge(y_lo, q + 1)
                            else:
                                pe.wait_ge(taken, b)
                        for c in range(2):
                            k = 2 * (2 * i + q // 2) + c
                            pe.wait_ge(d_lo, k + 1)
                            last = mm3(bank[q][:, :], wslot(slot, (2 * q + c) * P), hid(k), c == 0, c == 1)
                    last.then_inc(block_done, 1)
                pe.wait_ge(taken, B + POOL_OUT)
                pe.wait_ge(y_lo, 6)
                out_projection(l)

            pe.wait_ge(con_ready, 7)
            a = 0
            for l, (kind, _) in enumerate(plan.mixers):
                if kind == "nsa":
                    nsa(l, a)
                    a += 1
                elif kind == "sgu":
                    sgu(l)
                else:
                    pool(l)
                ffn(l)
            norm(plan.norms - 1)


def _tiles(w, nk=MT):
    K, M = w.shape
    b = w.reshape(K // P, P, M // P, P).transpose(2, 1, 0, 3).reshape(M // P, P, (K // P) * P)
    return _pad(b)


def _pad(b):
    return np.pad(b, ((0, 0), (0, 0), (0, BW - b.shape[2]))) if b.shape[2] < BW else b


def _pairs(w):
    return w.reshape(4, 2, P, S).transpose(0, 2, 1, 3).reshape(4, P, BW)


def _stream(i, mixers, total):
    out = []
    for l, (kind, j) in enumerate(mixers):
        if kind == "nsa":
            w = i["nsa_w_in"][j]
            kc, vc, ks, vs, kw, vw = [w[:, D + 256 * n:D + 256 * (n + 1)] for n in range(6)]
            out += [_tiles(np.ascontiguousarray(c)) for c in (kc, vc, ks, kw)]
            for c in "kv":
                w1 = i[f"nsa_cmp_{c}_w1"][j].reshape(2, 8, P, 2, P)
                out.append(w1.transpose(3, 0, 2, 1, 4).reshape(4, P, BW))
            k2, v2 = (i[f"nsa_cmp_{c}_w2"][j].reshape(2, P, DH) for c in "kv")
            out.append(_pad(np.concatenate([k2[0], k2[0], k2[1], k2[1], v2[0], v2[1]], axis=1)[None]))
            out.append(_tiles(w[:, 0:D]))
            gl = w[:, D + 1536:].reshape(MT, P, 3 * HEADS).transpose(1, 0, 2).reshape(1, P, MT * 3 * HEADS)
            out.append(_pad(gl))
            out.append(_pairs(np.concatenate([vs, vw], axis=1)))
            out.append(_tiles(i["nsa_w_out"][j]))
        elif kind == "sgu":
            w = i["sgu_w_in"][j]
            out += [_pairs(w[:, D + S * h:D + S * (h + 1)]) for h in range(2)]
            out.append(i["sgu_w_s"][j].transpose(2, 0, 1).reshape(1, P, BW))
            out.append(_tiles(w[:, 0:D]))
            out.append(_tiles(i["sgu_w_out"][j]))
        else:
            out.append(_tiles(i["pool_w_in"][j]))
            g = i["pool_w_grp"][j].reshape(2, 2, 2, P, 2, P)
            out.append(g.transpose(0, 3, 1, 4, 2, 5).reshape(2, P, BW))
            out.append(_tiles(i["pool_w_out"][j]))
        up, down = i["ffn_w_gate_up"][l], i["ffn_w_down"][l]
        gate, lin = (_tiles(up[:, h * HIDDEN_TILES * P:(h + 1) * HIDDEN_TILES * P]) for h in range(2))
        both = np.stack([gate, lin], axis=1)
        t = 0
        for n in PARTS:
            out.append(both[t:t + n].reshape(2 * n, P, BW))
            out.append(_tiles(down[t * P:(t + n) * P]))
            t += n
    have = sum(b.shape[0] for b in out)
    out.append(np.zeros((total - have, P, BW), np.float32))
    return np.concatenate(out)


def _params(i):
    par = np.zeros((P, PAR_COLS), np.float32)

    def put(name, v, at=0):
        par[:, PAR[name] + at:PAR[name] + at + v.shape[1]] = v

    def by_tile(v):
        return v.reshape(MT, P).T

    for n in range(4):
        put("gn", by_tile(i["mix_norm"][n]), 2 * n * MT)
        put("gn", by_tile(i["ffn_norm"][n]), (2 * n + 1) * MT)
    put("gn", by_tile(i["final_norm"]), 8 * MT)
    put("ln_g", by_tile(i["sgu_ln_g"][0]))
    put("ln_b", by_tile(i["sgu_ln_b"][0]))
    put("pool_scale", by_tile(i["pool_scale"][0]))
    for j in range(2):
        for v, c in enumerate("kv"):
            put("pos", i[f"nsa_cmp_pos_{c}"][j].reshape(16, P).T, 32 * j + 16 * v)
    d = np.arange(P) % DH
    half = ROPE_DIM // 2
    inv = ROPE_THETA ** (-np.arange(0, ROPE_DIM, 2, dtype=np.float64) / ROPE_DIM)
    put("invf", np.where(d < ROPE_DIM, inv[d % half], 0.0).astype(np.float32)[:, None])
    put("anyvalid", (np.arange(P) >= 31).astype(np.float32)[:, None])
    t = np.arange(POOL_PAD)
    for gi in range(4):
        w = 2 ** (gi + 1)
        put("corr", np.broadcast_to((w / np.minimum(t + 1, w)).astype(np.float32), (P, POOL_PAD)), gi * POOL_PAD)
    return par


def _consts():
    con = np.zeros((P, CON_COLS), np.float32)
    r = np.arange(P)
    con[:, CON["ident"]:CON["ident"] + P] = np.eye(P)
    half = ROPE_DIM // 2
    for h in (0, DH):
        for f in range(half):
            con[h + f + half, CON["swap"] + h + f] = -1.0
            con[h + f, CON["swap"] + h + f + half] = 1.0
    con[:, CON["causal"]:CON["causal"] + P] = np.where(r[None, :] > r[:, None], NEG, 0.0)
    con[:, CON["tril"]:CON["tril"] + P] = (r[None, :] >= r[:, None])
    n = np.arange(P) % NCMP
    for t in range(TT):
        ok = (16 * n[None, :] + 31 <= P * t + r[:, None]) & (n[None, :] < 31)
        con[:, CON["cmask"] + P * t:CON["cmask"] + P * (t + 1)] = np.where(ok, 0.0, NEG)
    con[:, CON["blk"]:CON["blk"] + 4] = (r[:, None] // NCMP == np.arange(4)[None, :])
    return con


def kernel(mixers=MIXERS, **inputs):
    import concourse.bacc as bacc
    from concourse.bass_utils import run_bass_kernel_spmd

    i = {k: np.asarray(v) for k, v in inputs.items()}
    plan = Plan(mixers)
    arrays = {
        "x_in": np.ascontiguousarray(i["x"][0].T.reshape(MT, P, S).transpose(1, 0, 2)),
        "positions": np.ascontiguousarray(i["positions"]),
        "stream": _stream(i, mixers, plan.stream),
        "params": _params(i),
        "consts": _consts(),
        "b_s": np.ascontiguousarray(i["sgu_b_s"][0].reshape(1, 8 * P)),
    }
    nc = bacc.Bacc("TRN2", target_bir_lowering=False, num_devices=1)
    args = [nc.dram_tensor(n, a.shape, mybir.dt.from_np(a.dtype), kind="ExternalInput").ap()
            for n, a in arrays.items()]
    out = nc.dram_tensor("out", (P, MT, S), F32, kind="ExternalOutput").ap()
    build(nc, *args, out, mixers=mixers)
    r = run_bass_kernel_spmd(nc, [arrays], core_ids=[0])
    y = r.results[0]["out"]
    return np.ascontiguousarray(y.transpose(1, 0, 2).reshape(D, S).T)[None]
```

```python
from contextlib import ExitStack

import numpy as np

import concourse.bass as bass
from concourse import mybir

F32 = mybir.dt.float32
F32R = mybir.dt.float32r
BF16 = mybir.dt.bfloat16
I32 = mybir.dt.int32
ALU = mybir.AluOpType
ACT = mybir.ActivationFunctionType
AX = mybir.AxisListType

P = 128
S = 512
D = 1024
MT = D // P
TT = S // P
HEADS, GROUPS, DH = 16, 4, 64
NCMP = 32
HIDDEN_TILES = 22
PARTS = (8, 8, 6)
BW = 1024
RING = 4
RAW = 2
AHEAD = RING - 1
KCW = S + 16
POOL_PAD = 16
RMS_EPS, LN_EPS, NEG = 1e-6, 1e-5, -1e30
ROPE_THETA, ROPE_DIM = 500000.0, 16

MIXERS = (("nsa", 0), ("sgu", 0), ("pool", 0), ("nsa", 1))
MIX_BLOCKS = {"nsa": 38, "sgu": 25, "pool": 18}
FFN_BLOCKS = 2 * HIDDEN_TILES + MT * len(PARTS)

(KC, VC, KS, KWIN, W1K, W1V, W2, Q, GATE, V, NSA_OUT) = (0, 2, 4, 6, 8, 12, 16, 17, 25, 26, 30)
SGU_V, SGU_WS, SGU_U, SGU_OUT = 0, 8, 9, 17
POOL_Z, POOL_GRP, POOL_OUT = 0, 8, 10

TWO_PI = (6.28125, 0.0019340515136718750, 1.2556659146e-6)
ROUND = 1.5 * 2.0 ** 23
PI_F = 3.1415925
ROPE_STEPS = 13

PAR = {}
_at = 0
for _name, _n in (("gn", 9 * MT), ("ln_g", MT), ("ln_b", MT), ("pool_scale", MT), ("pos", 2 * 2 * 16),
                  ("invf", 1), ("anyvalid", 1), ("corr", 4 * POOL_PAD)):
    PAR[_name] = _at
    _at += _n
PAR_COLS = _at
CON = {"ident": 0, "swap": 128, "causal": 256, "tril": 384, "cmask": 512, "end": 512 + TT * P}
CON_COLS = CON["end"]


class Plan:

    def __init__(self, mixers):
        self.mixers = mixers
        self.mix, self.ffn, self.nsa = [], [], []
        b = a = 0
        for kind, _ in mixers:
            self.mix.append(b)
            self.nsa.append(a)
            a += kind == "nsa"
            b += MIX_BLOCKS[kind]
            self.ffn.append(b)
            b += FFN_BLOCKS
        self.blocks = b
        self.stream = b + AHEAD + (b + AHEAD) % 2
        self.norms = 2 * len(mixers) + 1

    def out_block(self, l):
        kind = self.mixers[l][0]
        return self.mix[l] + {"nsa": NSA_OUT, "sgu": SGU_OUT, "pool": POOL_OUT}[kind]

    def part_block(self, l, p):
        up = self.ffn[l] + sum(2 * n + MT for n in PARTS[:p])
        return up, up + 2 * PARTS[p]

    def norm_blocks(self, n):
        return self.out_block(n // 2) if n % 2 else self.part_block(n // 2 - 1, 2)[1]


UNITS, PACKS = 9 * TT, 5 * TT
TURN = 3
SPLIT = TURN + 1
MULT = TURN + 3
LEAVE = MULT + 1


def ran(x, first):
    return x < UNITS and (x >= 0 or not first)


def pack_end(x):
    t, r = x // 9, x % 9
    return 5 * t + r // 2 if r % 2 == 0 else None


def pack_splits(c):
    w = P if c % 5 == 0 else 2 * P * (c % PACKS // 5 + 1)
    return [(i, min(S, w - S * i)) for i in range(-(-w // S))]


def splits_before(c):
    return sum(len(pack_splits(i)) for i in range(c)) if c >= 0 else splits_before(c + PACKS) - SPLITS


SPLITS = splits_before(PACKS)


def build(nc, x_in, positions, stream, params, consts, b_s, out, mixers=MIXERS):
    plan = Plan(mixers)
    ctx = ExitStack()
    with ctx:
        def sb(name, shape, dt):
            return ctx.enter_context(nc.sbuf_tensor(name, shape, dt))

        def sem(name):
            return ctx.enter_context(nc.semaphore(name))

        x = sb("x", [P, MT, S], F32)
        xs_hi = sb("xs_hi", [P, MT, S], F32R)
        xs_lo = sb("xs_lo", [P, MT, S], F32R)
        raw = sb("raw", [P, RAW, BW], F32)
        w_hi = sb("w_hi", [P, RING, BW], F32R)
        w_lo = sb("w_lo", [P, RING, BW], F32R)
        hid_hi = sb("hid_hi", [P, MT, S], F32R)
        hid_lo = sb("hid_lo", [P, MT, S], F32R)
        mix_hi = sb("mix_hi", [P, MT, S], F32R)
        mix_lo = sb("mix_lo", [P, MT, S], F32R)
        big = sb("big", [P, 2 * GROUPS * KCW], F32)
        tmp = sb("tmp", [P, 4, S], F32)
        rstat = sb("rstat", [P, S + 2 * TT], F32)
        vstat = sb("vstat", [P, S + 2 * TT], F32)
        work = sb("work", [P, 2, S], F32)
        work2 = sb("work2", [P, 2, S], F32)
        rope = sb("rope", [P, 2, S], F32)
        sm_hi = sb("sm_hi", [P, GROUPS, 4 * DH], F32R)
        sm_lo = sb("sm_lo", [P, GROUPS, 4 * DH], F32R)
        par = sb("par", [P, PAR_COLS], F32)
        ident = sb("ident", [P, P], F32)
        tril = sb("tril", [P, P], BF16)
        ones = sb("ones", [P, P], F32R)
        swap = sb("swap", [P, P], F32R)
        ident_b = sb("ident_b", [P, P], BF16)
        causal_b = sb("causal_b", [P, P], BF16)
        cmask_b = sb("cmask_b", [P, TT, P], BF16)
        kc_hi = sb("kc_hi", [P, P], F32R)
        kc_lo = sb("kc_lo", [P, P], F32R)
        vc_hi = sb("vc_hi", [P, DH], F32R)
        vc_lo = sb("vc_lo", [P, DH], F32R)
        gates = sb("gates", [P, TT, 3, HEADS], F32)
        nmax = sb("nmax", [P, 4, 4], F32)
        den = sb("den", [P, 4], F32)
        cden = sb("cden", [P, 2, 4], F32)
        bnst = sb("bnst", [P, TT, 2, 6], F32)
        mv = sb("mv", [P, TT, 2], F32)
        lstd = sb("lstd", [P, 4, TT], F32)

        bank = [ctx.enter_context(nc.psum_tensor(f"bank{i}", [P, S], F32)) for i in range(8)]

        q_st = xs_hi[:, 0:4, :]
        q_by_half = q_st.rearrange("p (jj h) t -> p h jj t", h=2)
        vs_hi = xs_hi[:, 4:6, :].rearrange("p a (k c) -> p (a k) c", k=2).rearrange(
            "p t (b h d) -> p t b h d", b=2, h=2)
        vs_lo = xs_hi[:, 6:8, :].rearrange("p a (k c) -> p (a k) c", k=2).rearrange(
            "p t (b h d) -> p t b h d", b=2, h=2)
        pt_hi = xs_lo[:, 0:4, :]
        pt_lo = xs_lo[:, 4:8, :]
        val = tmp
        prob = [w[:, k, :] for w in (work, work2) for k in range(2)]
        vcr_hi = sm_hi[:, 2:3, :].rearrange("p o (g d) -> p (o g) d", g=GROUPS)
        vcr_lo = sm_lo[:, 2:3, :].rearrange("p o (g d) -> p (o g) d", g=GROUPS)
        vcs_hi = sm_hi[:, 0:2, :].rearrange("p a (k h d) -> p (a k) h d", k=2, h=2)
        vcs_lo = sm_lo[:, 0:2, :].rearrange("p a (k h d) -> p (a k) h d", k=2, h=2)
        key_hi = hid_hi[:, :, :].rearrange("p (r g) t -> p r g t", r=2)
        key_lo = hid_lo[:, :, :].rearrange("p (r g) t -> p r g t", r=2)
        cm_hi = mix_hi[:, :, :].rearrange("p (v k) t -> p v (k t)", v=2)
        cm_lo = mix_lo[:, :, :].rearrange("p (v k) t -> p v (k t)", v=2)
        kc2 = big[:, :].rearrange("p (v g t) -> p v g t", v=2, g=GROUPS)
        qf = big[:, 0:MT * S].rearrange("p (m t) -> p m t", m=MT)
        sgu_v = big[:, 0:TT * D].rearrange("p (t c) -> p t c", t=TT)
        sq_hi = sm_hi[:, 0:2, :].rearrange("p a b -> p (a b)")
        sq_lo = sm_lo[:, 0:2, :].rearrange("p a b -> p (a b)")
        ch_hi = sm_hi[:, 2:4, :].rearrange("p a (b n) -> p (a b) n", b=2)
        ch_lo = sm_lo[:, 2:4, :].rearrange("p a (b n) -> p (a b) n", b=2)
        vc_f = tmp[:, 3, 0:DH]
        ws_hi = sm_hi[:, :, :].rearrange("p a b -> p (a b)")
        ws_lo = sm_lo[:, :, :].rearrange("p a b -> p (a b)")
        bias_t = work[:, :, :].rearrange("p a b -> p (a b)")
        bs_t = work2[:, :, :].rearrange("p a b -> p (a b)")
        v_hi = hid_hi[:, :, :].rearrange("p m t -> p (m t)").rearrange("p (t c) -> p t c", t=TT)
        v_lo = hid_lo[:, :, :].rearrange("p m t -> p (m t)").rearrange("p (t c) -> p t c", t=TT)
        con = big[:, 0:CON_COLS]
        diag = vstat[:, 0:4 * P].rearrange("p (k n) -> p k n", k=4)
        rrow, rcol = rstat[:, 0:S], rstat[:, S:S + 2 * TT].rearrange("p (t c) -> p t c", c=2)

        def f32(ap):
            return ap.bitcast(F32)

        def tile(t, m):
            return t[:, m, :] if type(m) is int else t[:, bass.ds(m, 1), :].rearrange("p o t -> p (o t)")

        def g_of(n, m):
            return par[:, bass.ds(PAR["gn"] + n * MT + m, 1)]

        def col(name, i):
            return par[:, PAR[name] + i:PAR[name] + i + 1]

        raw_full = [sem(f"raw_full{i}") for i in range(RAW)]
        par_full, con_full, pos_full, x_full, bs_full = (sem(n) for n in (
            "par_full", "con_full", "pos_full", "x_full", "bs_full"))
        out_done = sem("out_done")
        w_hi_ready, w_lo_ready = sem("w_hi_ready"), sem("w_lo_ready")
        block_done = sem("block_done")
        taken = sem("taken")
        xs_hi_ready, xs_lo_ready = sem("xs_hi_ready"), sem("xs_lo_ready")
        sq_step = sem("sq_step")
        sq_hi_ready, sq_lo_ready = sem("sq_hi_ready"), sem("sq_lo_ready")
        norm_sum, var_ready, std_ready, norm_step = (sem(n) for n in (
            "norm_sum", "var_ready", "std_ready", "norm_step"))
        silu_ready, hid_full = sem("silu_ready"), sem("hid_full")
        hid_hi_ready, hid_lo_ready = sem("hid_hi_ready"), sem("hid_lo_ready")
        con_ready, ones_ready, rope_step, rope_sin = (sem(n) for n in (
            "con_ready", "ones_ready", "rope_step", "rope_sin"))
        tab_ready = sem("tab_ready")
        rq_hi_ready, rq_lo_ready, swapped, rot_b, rotated = (sem(n) for n in (
            "rq_hi_ready", "rq_lo_ready", "swapped", "rot_b", "rotated"))
        kc_rows, key_hi_ready, key_lo_ready = sem("kc_rows"), sem("key_hi_ready"), sem("key_lo_ready")
        kc_pad = sem("kc_pad")
        cm_full, cm_hi_ready, cm_lo_ready = sem("cm_full"), sem("cm_hi_ready"), sem("cm_lo_ready")
        ch_full, ch_hi_ready = sem("ch_full"), sem("ch_hi_ready")
        kcmp_hi, vcmp_full, vcmp_hi, vcmp_lo = (sem(n) for n in ("kcmp_hi", "vcmp_full", "vcmp_hi", "vcmp_lo"))
        vcr_ready, vcs_zero = sem("vcr_ready"), sem("vcs_zero")
        gate_turned, gate_ready, gate_masked = sem("gate_turned"), sem("gate_ready"), sem("gate_masked")
        q_hi_ready, q_lo_ready = sem("q_hi_ready"), sem("q_lo_ready")
        score_ready, max_ready, cmax_ready, prob_ready, csum_ready, recip_ready = (sem(n) for n in (
            "score_ready", "max_ready", "cmax_ready", "prob_ready", "csum_ready", "recip_ready"))
        cwgt_ready, diag_ready = sem("cwgt_ready"), sem("diag_ready")
        prob_t, pt_hi_ready, pt_lo_ready, pv_done = (sem(n) for n in (
            "prob_t", "pt_hi_ready", "pt_lo_ready", "pv_done"))
        vs_hi_ready, vs_lo_ready, vcs_hi_ready, vcs_lo_ready, o_hi_ready, o_lo_ready = (sem(n) for n in (
            "vs_hi_ready", "vs_lo_ready", "vcs_hi_ready", "vcs_lo_ready", "o_hi_ready", "o_lo_ready"))
        v_gelu, ln_step, ln_var, ln_std, vn_ready, vn_hi, vn_lo = (sem(n) for n in (
            "v_gelu", "ln_step", "ln_var", "ln_std", "vn_ready", "vn_hi", "vn_lo"))
        ws_masked, bias_ready, u_gelu, mixed, sv_ready, mix_full, mix_hi_ready, mix_lo_ready = (
            sem(n) for n in ("ws_masked", "bias_ready", "u_gelu", "mixed", "sv_ready", "mix_full",
                             "mix_hi_ready", "mix_lo_ready"))
        pool_step, d_full, d_hi, d_lo, y_hi, y_lo, z_pad = (sem(n) for n in (
            "pool_step", "d_full", "d_hi", "d_lo", "y_hi", "y_lo", "z_pad"))
        y_out = sem("y_out")

        norm_of_mixer = lambda l: 2 * l
        norm_of_ffn = lambda l: 2 * l + 1

        def wait_past(eng, sem_, value):
            if not (type(value) is int and value <= 0):
                eng.wait_ge(sem_, value)

        def wait_x(eng, n, m):
            if n == 0:
                eng.wait_ge(x_full, 16)
            else:
                eng.wait_ge(taken, plan.norm_blocks(n) + m + 1)

        block = ctx.enter_context(nc.Block())

        @block.sync
        def _(sp):
            sp.dma_start(par[:, :], params).then_inc(par_full, 16)
            sp.dma_start(raw[:, 0, :], stream[0]).then_inc(raw_full[0], 16)
            sp.dma_start(x[:, :, :], x_in).then_inc(x_full, 16)
            sp.dma_start(raw[:, 1, :], stream[1]).then_inc(raw_full[1], 16)
            sp.dma_start(con, consts).then_inc(con_full, 16)
            sp.dma_start(tmp[:, 0, :].bitcast(I32), positions.partition_broadcast(P)).then_inc(pos_full, 16)

            def load(b, k):
                sp.wait_ge(w_lo_ready, b - RAW + 1)
                sp.dma_start(raw[:, k, :], stream[b]).then_inc(raw_full[k], 16)

            with sp.Fori(1, plan.stream // RAW) as i:
                for k in range(RAW):
                    load(i * RAW + k, k)
            for m in range(MT):
                sp.wait_ge(y_out, m + 1)
                sp.dma_start(out[:, m, :], qf[:, m, :]).then_inc(out_done, 16)
            sp.wait_ge(out_done, 16 * MT)

        @block.gpsimd
        def _(gp):
            def squares(n):
                base = (2 * MT - 1) * n
                wait_x(gp, n, 0)
                if n:
                    gp.wait_ge(norm_step, 5 * n)
                gp.tensor_tensor(work[:, 0, :], x[:, 0, :], x[:, 0, :], ALU.mult).then_inc(sq_step, 1)
                with gp.Fori(1, MT) as m:
                    wait_x(gp, n, m)
                    gp.wait_ge(sq_step, 2 * m + base - 1)
                    gp.tensor_tensor(work2[:, 0, :], tile(x, m), tile(x, m), ALU.mult).then_inc(sq_step, 1)
                    gp.wait_ge(sq_step, 2 * m + base)
                    gp.tensor_tensor(work[:, 0, :], work[:, 0, :], work2[:, 0, :], ALU.add).then_inc(sq_step, 1)

            def nsa(l, a):
                for c in range(8):
                    v, k0 = c // 4, 4 * (c % 4)
                    gp.wait_ge(kc_rows, 16 * a + 8 * (v + 1))
                    rows = bass.AP(tensor=big, offset=v * GROUPS * KCW + 2 * k0,
                                   ap=[[2 * GROUPS * KCW, P], [2, 4], [KCW, GROUPS], [16, NCMP]])
                    at = PAR["pos"] + 32 * plan.mixers[l][1] + 16 * v + k0
                    bias = bass.AP(tensor=par, offset=at, ap=[[PAR_COLS, P], [1, 4], [0, GROUPS], [0, NCMP]])
                    wait_past(gp, cm_lo_ready, 8 * a + c)
                    nc.gpsimd.tensor_tensor(tmp[:, 3, :].rearrange("p (k g n) -> p k g n", k=4, g=GROUPS), rows,
                                            bias, ALU.add).then_inc(cm_full, 1)

                gp.wait_ge(vcmp_lo, a + 1)
                for g in range(GROUPS):
                    for j in range(4):
                        for dst, src in ((vcr_hi, vc_hi), (vcr_lo, vc_lo)):
                            nc.gpsimd.tensor_copy(dst[32 * j:32 * j + 32, g, :], f32(src[32 * g:32 * g + 32, :])
                                                  ).then_inc(vcr_ready, 1)

                gp.wait_ge(block_done, plan.mix[l] + GATE)
                gp.wait_ge(swapped, 14 * (a + 1))
                gp.wait_ge(vcr_ready, 32 * (a + 1))
                gp.memset(sm_hi[:, 0:2, :].bitcast(F32), 0.0).then_inc(vcs_zero, 1)
                gp.memset(sm_lo[:, 0:2, :].bitcast(F32), 0.0).then_inc(vcs_zero, 1)

            squares(0)
            a = 0
            for l, (kind, _) in enumerate(plan.mixers):
                if kind == "nsa":
                    nsa(l, a)
                    a += 1
                squares(norm_of_ffn(l))
                squares(norm_of_ffn(l) + 1)

        @block.scalar
        def _(act):
            def split(b, slot=None):
                slot = b % RING if slot is None else slot
                k = slot % RAW
                nth = (b - k) // RAW if type(b) is int else None
                act.wait_ge(raw_full[k], 16 * (nth + 1) if nth is not None else (b - k) * 8 + 16)
                if not (type(b) is int and b < RING):
                    act.wait_ge(block_done, b - RING + 1)
                nc.scalar.activation(w_hi[:, slot, :], raw[:, k, :], ACT.Copy).then_inc(w_hi_ready, 1)

            def split_after(b, slot):
                split(b + AHEAD, (slot + AHEAD) % RING)

            def xs_high(n, m):
                wait_x(act, n, m)
                nc.scalar.activation(tile(xs_hi, m), tile(x, m), ACT.Copy, scale=g_of(n, m)).then_inc(xs_hi_ready, 1)

            def sum_split(n):
                act.wait_ge(sq_step, (2 * MT - 1) * (n + 1))
                nc.scalar.activation(sq_hi, work[:, 0, :], ACT.Copy).then_inc(sq_hi_ready, 1)

            def root(n):
                act.wait_ge(var_ready, 2 * (n + 1))
                nc.scalar.activation(rstat[:, :], vstat[:, :], ACT.Sqrt).then_inc(std_ready, 1)

            def out_projection(l):
                n, b0 = norm_of_ffn(l), plan.out_block(l)
                s0 = b0 % RING
                with act.Fori(0, MT // RING) as i:
                    for k in range(RING):
                        split_after(i * RING + (b0 + k), (s0 + k) % RING)
                        xs_high(n, i * RING + k)

            def ffn(l):
                n = norm_of_ffn(l)

                def hidden_tile(t, b, slot, first=False):
                    split_after(b, slot)
                    if first:
                        root(n)
                    act.wait_ge(taken, b + 1)
                    nc.scalar.activation(tmp[:, 1, :], tmp[:, 0, :], ACT.Silu).then_inc(silu_ready, 1)
                    split_after(b + 1, (slot + 1) % RING)
                    act.wait_ge(hid_full, t + 1)

                for p, tiles in enumerate(PARTS):
                    up, down = plan.part_block(l, p)
                    s0 = up % RING
                    t0 = HIDDEN_TILES * l + 8 * p

                    def pair(i):
                        for k in range(2):
                            hidden_tile(i * 2 + (t0 + k), i * 4 + (up + 2 * k), (s0 + 2 * k) % RING,
                                 p == 0 and k == 0 and type(i) is int)
                            nc.scalar.activation(hid_hi[:, bass.ds(i * 2 + k, 1), :], tmp[:, 3:4, :], ACT.Copy
                                                 ).then_inc(hid_hi_ready, 1)

                    first = 0
                    if p == 0:
                        sum_split(n)
                        pair(0)
                        first = 1
                    with act.Fori(first, tiles // 2) as i:
                        pair(i)
                    s0d = down % RING
                    with act.Fori(0, MT // RING) as i:
                        for k in range(RING):
                            split_after(i * RING + (down + k), (s0d + k) % RING)
                            if p == len(PARTS) - 1 and n + 1 < plan.norms - 1:
                                xs_high(n + 1, i * RING + k)

            def rope_high(b, slot, rho):
                act.wait_ge(block_done, b + 1)
                if not (type(rho) is int and rho == 0):
                    act.wait_ge(swapped, rho)
                nc.scalar.activation(sm_hi[:, 0:2, :].rearrange("p a b -> p (a b)"), bank[slot][:, :], ACT.Copy
                                     ).then_inc(rq_hi_ready, 1)

            def nsa(l, a):
                B = plan.mix[l]
                n = norm_of_mixer(l)

                def post(j):
                    rt = tmp[:, j % 2, :]
                    if j in (VC, VC + 1):
                        act.wait_ge(taken, B + j + 1)
                    else:
                        rho = j if j < 2 else j - 2
                        act.wait_ge(rotated, 14 * a + rho + 1)
                    for half in range(2):
                        g = 2 * (j % 2) + half
                        src = rt[64 * half:64 * half + 64, :]
                        if j < KS:
                            if half == 0 and j == 0:
                                act.wait_ge(kc_pad, 2 * (a + 1))
                            v = j // 2
                            nc.scalar.activation(kc2[0:64, v, g, 0:S], src, ACT.Copy).then_inc(kc_rows, 1)
                            nc.scalar.activation(kc2[64:128, v, g, 0:S - 1], src[:, 1:S], ACT.Copy
                                                 ).then_inc(kc_rows, 1)
                        else:
                            r = (j - KS) // 2
                            for h in (half, 1 - half):
                                nc.scalar.activation(key_hi[64 * h:64 * h + 64, r, g, :], src, ACT.Copy
                                                     ).then_inc(key_hi_ready, 1)

                def cm_high(c):
                    act.wait_ge(cm_full, 8 * a + c + 1)
                    nc.scalar.activation(cm_hi[:, c // 4, bass.ts(c % 4, S)], tmp[:, 3, :], ACT.Copy
                                         ).then_inc(cm_hi_ready, 1)

                sum_split(n)
                for j in range(W1K):
                    b, slot = B + j, (B + j) % RING
                    split_after(b, slot)
                    if j == 0:
                        root(n)
                    if j not in (VC, VC + 1):
                        rope_high(b, slot, 14 * a + (j if j < 2 else j - 2))
                    if j:
                        post(j - 1)
                    if j >= 4:
                        cm_high(j - 4)
                post(W1K - 1)
                for j in range(W1K, W2):
                    b, slot = B + j, (B + j) % RING
                    split_after(b, slot)
                    if j < W1K + 4:
                        cm_high(j - W1K + 4)
                    if j % 2:
                        q = (j - W1K) // 2
                        act.wait_ge(block_done, b + 1)
                        nc.scalar.activation(tmp[:, 2, bass.ts(q, P)], bank[(slot - 1) % RING][:, 0:P],
                                             ACT.Gelu_apprx_tanh).then_inc(ch_full, 1)
                        act.wait_ge(ch_full, 4 * a + q + 1)
                        nc.scalar.activation(ch_hi[:, q, :], tmp[:, 2, bass.ts(q, P)], ACT.Copy
                                             ).then_inc(ch_hi_ready, 1)
                b, slot = B + W2, (B + W2) % RING
                split_after(b, slot)
                act.wait_ge(block_done, b + 1)
                nc.scalar.activation(kc_hi[:, :], bank[slot][:, 0:P], ACT.Copy).then_inc(kcmp_hi, 1)
                nc.scalar.activation(vc_f, bank[6][:, 0:DH], ACT.Copy).then_inc(vcmp_full, 1)
                act.wait_ge(vcmp_full, a + 1)
                nc.scalar.activation(vc_hi[:, :], vc_f, ACT.Copy).then_inc(vcmp_hi, 1)

                with act.Fori(0, 2) as i:
                    for k in range(RING):
                        slot = (B + Q + k) % RING
                        b = i * RING + (B + Q + k)
                        split_after(b, slot)
                        rope_high(b, slot, i * RING + (14 * a + 6 + k))
                split_after(B + GATE, (B + GATE) % RING)
                for j in range(4):
                    if j == 3:
                        act.wait_ge(gate_turned, a + 1)
                        for t in range(TT):
                            nc.scalar.activation(gates[:, t, :, :].rearrange("p a b -> p (a b)"),
                                                 bank[6][:, P * t:P * t + 3 * HEADS], ACT.Sigmoid,
                                                 scale=rcol[:, t, 0:1]).then_inc(gate_ready, 1)
                    split_after(B + V + j, (B + V + j) % RING)
                act.wait_ge(block_done, B + V + 4)
                attention(l, a)
                out_projection(l)

            def attention(l, a):
                def queries_high(g, t):
                    for h in range(2):
                        nc.scalar.activation(q_by_half[64 * h:64 * h + 64, h, :, bass.ts(t, P)],
                                             qf[64 * h:64 * h + 64, bass.ds(g * 2, 2), bass.ts(t, P)],
                                             ACT.Copy, scale=DH ** -0.5).then_inc(q_hi_ready, 1)

                def values_high(g, t):
                    for br in range(2):
                        v = val[:, t, bass.ds((g + 4 * br) * DH, DH)].unsqueeze(1).broadcast_to([P, 2, DH])
                        nc.scalar.activation(vs_hi[:, t, br, :, :], v, ACT.Copy).then_inc(vs_hi_ready, 1)

                def steps(g, begin, end, first):
                    for s in range(begin, end):
                        c = pack_end(s - SPLIT)
                        if ran(s - SPLIT, first) and c is not None:
                            act.wait_ge(prob_t, g * UNITS + (TT * UNITS * a + s - SPLIT + 1))
                            wait_past(act, pv_done, g * PACKS + (TT * PACKS * a + c - 1))
                            for i, w in pack_splits(c):
                                k = 2 * (c % 2) + i
                                nc.scalar.activation(pt_hi[:, k, 0:w], bank[2 + k][:, 0:w], ACT.Copy
                                                     ).then_inc(pt_hi_ready, 1)
                        if s == 0:
                            wait_past(act, score_ready, g * UNITS + TT * UNITS * a)
                            queries_high(g, 0)
                        if s < UNITS:
                            u = g * UNITS + (TT * UNITS * a + s)
                            width = P if s % 9 == 0 else P * (s // 9 + 1)
                            act.wait_ge(max_ready, u + 1)
                            if s % 9 == 0:
                                nc.scalar.activation(prob[s % 4][:, 0:P], prob[s % 4][:, 0:P], ACT.Exp
                                                     ).then_inc(prob_ready, 1)
                            else:
                                wait_past(act, prob_t, u - 3)
                                nc.scalar.activation(prob[s % 4][:, 0:width], bank[s % 2][:, 0:width], ACT.Exp,
                                                     bias=nmax[:, s % 4, 0:1], accum_out=den[:, s % 4:s % 4 + 1]
                                                     ).then_inc(prob_ready, 1)
                        if s == 2:
                            wait_past(act, pv_done, g * PACKS + (TT * PACKS * a - 4))
                            act.wait_ge(vcr_ready, 32 * (a + 1))
                            act.wait_ge(vcs_zero, 2 * (a + 1))
                            for j in range(4):
                                row = slice(NCMP * j, NCMP * j + NCMP)
                                vc = f32(vcr_hi[row, bass.ds(g, 1), :]).broadcast_to([NCMP, 2, DH])
                                nc.scalar.activation(vcs_hi[row, j, :, :], vc, ACT.Copy).then_inc(vcs_hi_ready, 1)
                        if s == MULT:
                            wait_past(act, pv_done, g * PACKS + TT * PACKS * a)
                            act.wait_ge(taken, plan.mix[l] + NSA_OUT)
                            values_high(g, 0)
                        if s % 9 == 5 and s < 9 * (TT - 1):
                            queries_high(g, s // 9 + 1)
                        if s % 9 == 8 and s < 9 * (TT - 1):
                            values_high(g, s // 9 + 1)
                        x = s - LEAVE
                        if ran(x, first) and x % 9 == 8:
                            t = x % UNITS // 9
                            act.wait_ge(pv_done, g * PACKS + (TT * PACKS * a + 5 * (x // 9 + 1)))
                            for h in range(2):
                                nc.scalar.activation(
                                    mix_hi[64 * h:64 * h + 64, bass.ds(g * 2 + 2 * (x // UNITS), 2), bass.ts(t, P)],
                                    bank[6 + t % 2][64 * h:64 * h + 64, :].rearrange(
                                        "p (jj h q) -> p h jj q", jj=2, h=2)[:, h, :, :], ACT.Copy
                                ).then_inc(o_hi_ready, 1)

                steps(0, 0, UNITS, True)
                with act.Fori(1, GROUPS) as g:
                    steps(g, 0, UNITS, False)
                steps(GROUPS - 1, UNITS, UNITS + LEAVE, False)

            def sgu(l):
                B = plan.mix[l]
                sum_split(norm_of_mixer(l))
                for half in range(2):
                    for j in range(4):
                        b = B + 4 * half + j
                        split_after(b, b % RING)
                        if half == 0 and j == 0:
                            root(norm_of_mixer(l))
                            act.dma_start(bs_t, b_s.partition_broadcast(P)).then_inc(bs_full, 16)
                            act.wait_ge(norm_step, 5 * (norm_of_mixer(l) + 1))
                    act.wait_ge(block_done, B + 4 * half + 4)
                    for t in range(TT):
                        nc.scalar.activation(sgu_v[:, t, bass.ts(half, S)], bank[(B + t) % RING][:, :],
                                             ACT.Gelu_apprx_tanh, scale=rcol[:, t, 0:1]).then_inc(v_gelu, 1)
                split_after(B + SGU_WS, (B + SGU_WS) % RING)
                act.wait_ge(ln_var, 1)
                nc.scalar.activation(lstd[:, 1, :], lstd[:, 0, :], ACT.Sqrt).then_inc(ln_std, 1)
                for t in range(TT):
                    act.wait_ge(vn_ready, t + 1)
                    nc.scalar.activation(v_hi[:, t, :], sgu_v[:, t, :], ACT.Copy).then_inc(vn_hi, 1)
                    if t < 3:
                        split_after(B + SGU_U + t, (B + SGU_U + t) % RING)
                for m in range(MT):
                    if m + 3 < MT:
                        split_after(B + SGU_U + m + 3, (B + SGU_U + m + 3) % RING)
                    act.wait_ge(taken, B + SGU_U + m + 1)
                    nc.scalar.activation(tmp[:, 1, :], tmp[:, 0, :], ACT.Gelu_apprx_tanh).then_inc(u_gelu, 1)
                    act.wait_ge(mix_full, m + 1)
                    nc.scalar.activation(mix_hi[:, m, :], tmp[:, 3, :], ACT.Copy).then_inc(mix_hi_ready, 1)
                out_projection(l)

            def pool(l):
                B = plan.mix[l]
                sum_split(norm_of_mixer(l))
                for m in range(MT):
                    split_after(B + m, (B + m) % RING)
                    if m == 0:
                        root(norm_of_mixer(l))
                    act.wait_ge(d_full, m + 1)
                    nc.scalar.activation(hid_hi[:, m, :], tmp[:, 3, :], ACT.Copy).then_inc(d_hi, 1)
                for i in range(2):
                    b = B + POOL_GRP + i
                    split_after(b, b % RING)
                    act.wait_ge(block_done, b + 1)
                    for q in range(4):
                        m = 4 * i + q
                        nc.scalar.activation(mix_hi[:, m, :], bank[q][:, :], ACT.Copy, scale=col("pool_scale", m)
                                             ).then_inc(y_hi, 1)
                out_projection(l)

            split(0)
            act.wait_ge(par_full, 16)
            for m in range(MT):
                xs_high(0, m)
            for b in range(1, AHEAD):
                split(b)
            act.wait_ge(con_full, 16)
            nc.scalar.activation(ident[:, :], con[:, CON["ident"]:CON["ident"] + P], ACT.Copy).then_inc(con_ready, 1)
            nc.scalar.activation(tril[:, :], con[:, CON["tril"]:CON["tril"] + P], ACT.Copy).then_inc(con_ready, 1)
            nc.scalar.activation(swap[:, :], con[:, CON["swap"]:CON["swap"] + P], ACT.Copy).then_inc(con_ready, 1)
            nc.scalar.activation(ident_b[:, :], con[:, CON["ident"]:CON["ident"] + P], ACT.Copy
                                 ).then_inc(con_ready, 1)
            nc.scalar.activation(causal_b[:, :], con[:, CON["causal"]:CON["causal"] + P], ACT.Copy
                                 ).then_inc(con_ready, 1)
            nc.scalar.activation(cmask_b[:, :, :].rearrange("p a b -> p (a b)"),
                                 con[:, CON["cmask"]:CON["cmask"] + TT * P], ACT.Copy).then_inc(con_ready, 1)
            act.wait_ge(rope_step, ROPE_STEPS)
            nc.scalar.activation(rope[:, 1, :], tmp[:, 1, :], ACT.Sin).then_inc(rope_sin, 1)
            nc.scalar.activation(rope[:, 0, :], tmp[:, 2, :], ACT.Sin).then_inc(rope_sin, 1)
            a = 0
            for l, (kind, _) in enumerate(plan.mixers):
                if kind == "nsa":
                    nsa(l, a)
                    a += 1
                elif kind == "sgu":
                    sgu(l)
                else:
                    pool(l)
                ffn(l)
            sum_split(plan.norms - 1)
            root(plan.norms - 1)

        @block.vector
        def _(dve):
            def split(b, slot):
                k = slot % RAW
                dve.wait_ge(w_hi_ready, b + 1)
                nc.vector.tensor_tensor(w_lo[:, slot, :], raw[:, k, :], f32(w_hi[:, slot, :]), ALU.subtract
                                        ).then_inc(w_lo_ready, 1)

            def split_after(b, slot):
                split(b + AHEAD, (slot + AHEAD) % RING)

            def xs_low(n, m, at):
                dve.wait_ge(xs_hi_ready, at + 1)
                nc.vector.scalar_tensor_tensor(out=tile(xs_lo, m), in0=tile(x, m), scalar=g_of(n, m),
                                               in1=f32(tile(xs_hi, m)), op0=ALU.mult, op1=ALU.subtract
                                               ).then_inc(xs_lo_ready, 1)

            def sum_split(n):
                dve.wait_ge(sq_hi_ready, n + 1)
                nc.vector.tensor_tensor(sq_lo, work[:, 0, :], f32(sq_hi), ALU.subtract).then_inc(sq_lo_ready, 1)

            def rsqrt_steps(v, y, t, sem_, base):
                nc.vector.reciprocal(y, y).then_inc(sem_, 1)
                dve.wait_ge(sem_, base + 1)
                nc.vector.tensor_tensor(t, y, y, ALU.mult).then_inc(sem_, 1)
                dve.wait_ge(sem_, base + 2)
                nc.vector.tensor_tensor(t, t, v, ALU.mult).then_inc(sem_, 1)
                dve.wait_ge(sem_, base + 3)
                nc.vector.tensor_scalar(t, t, -0.5, 1.5, ALU.mult, ALU.add).then_inc(sem_, 1)
                dve.wait_ge(sem_, base + 4)
                nc.vector.tensor_tensor(y, y, t, ALU.mult).then_inc(sem_, 1)
                dve.wait_ge(sem_, base + 5)

            def norm(n):
                dve.wait_ge(norm_sum, n + 1)
                nc.vector.tensor_scalar(vstat[:, 0:S], bank[4][:, :], 1.0 / D, RMS_EPS, ALU.mult, ALU.add
                                        ).then_inc(var_ready, 1)
                nc.vector.tensor_scalar(vstat[:, S:S + 2 * TT], bank[5][:, 0:2 * TT], 1.0 / D, RMS_EPS, ALU.mult,
                                        ALU.add).then_inc(var_ready, 1)
                dve.wait_ge(std_ready, n + 1)
                both = work[:, :, :].rearrange("p a b -> p (a b)")[:, 0:S + 2 * TT]
                rsqrt_steps(vstat[:, :], rstat[:, :], both, norm_step, 5 * n)

            def add_residual(m, b, slot):
                dve.wait_ge(block_done, b + 1)
                nc.vector.tensor_tensor(tile(x, m), bank[slot][:, :], tile(x, m), ALU.add).then_inc(taken, 1)

            def out_projection(l):
                n, b0 = norm_of_ffn(l), plan.out_block(l)
                s0 = b0 % RING
                with dve.Fori(0, MT // RING) as i:
                    for k in range(RING):
                        b, slot, m = i * RING + (b0 + k), (s0 + k) % RING, i * RING + k
                        split_after(b, slot)
                        add_residual(m, b, slot)
                        dve.wait_ge(taken, b + 1)
                        xs_low(n, m, m + MT * n)

            def ffn(l):
                n = norm_of_ffn(l)
                last = n + 1 == plan.norms - 1
                for p, tiles in enumerate(PARTS):
                    up, down = plan.part_block(l, p)
                    s0 = up % RING
                    t0 = HIDDEN_TILES * l + 8 * p

                    def pair(i):
                        for k in range(2):
                            t, b, slot = i * 2 + (t0 + k), i * 4 + (up + 2 * k), (s0 + 2 * k) % RING
                            split_after(b, slot)
                            if p == 0 and k == 0 and type(i) is int:
                                norm(n)
                            dve.wait_ge(block_done, b + 1)
                            nc.vector.tensor_tensor(tmp[:, 0, :], bank[slot][:, :], rrow, ALU.mult
                                                    ).then_inc(taken, 1)
                            split_after(b + 1, (slot + 1) % RING)
                            dve.wait_ge(block_done, b + 2)
                            nc.vector.tensor_tensor(tmp[:, 2, :], bank[(slot + 1) % RING][:, :], rrow, ALU.mult
                                                    ).then_inc(taken, 1)
                            dve.wait_ge(taken, b + 2)
                            dve.wait_ge(silu_ready, t + 1)
                            nc.vector.tensor_tensor(tmp[:, 3, :], tmp[:, 1, :], tmp[:, 2, :], ALU.mult
                                                    ).then_inc(hid_full, 1)
                            dve.wait_ge(hid_full, t + 1)
                            dve.wait_ge(hid_hi_ready, t + 1)
                            h = bass.ds(i * 2 + k, 1)
                            nc.vector.tensor_tensor(hid_lo[:, h, :], tmp[:, 3:4, :], f32(hid_hi[:, h, :]),
                                                    ALU.subtract).then_inc(hid_lo_ready, 1)

                    first = 0
                    if p == 0:
                        sum_split(n)
                        pair(0)
                        first = 1
                    with dve.Fori(first, tiles // 2) as i:
                        pair(i)
                    s0d = down % RING
                    with dve.Fori(0, MT // RING) as i:
                        for k in range(RING):
                            b, slot, m = i * RING + (down + k), (s0d + k) % RING, i * RING + k
                            split_after(b, slot)
                            dve.wait_ge(taken, b)
                            add_residual(m, b, slot)
                            if p == len(PARTS) - 1 and not last:
                                dve.wait_ge(taken, b + 1)
                                xs_low(n + 1, m, m + MT * (n + 1))

            def nsa(l, a):
                B = plan.mix[l]
                n = norm_of_mixer(l)

                def rope_low(b, slot, rho):
                    dve.wait_ge(rq_hi_ready, rho + 1)
                    nc.vector.tensor_tensor(sq_lo, bank[slot][:, :], f32(sq_hi), ALU.subtract
                                            ).then_inc(rq_lo_ready, 1)

                def rotate(b, slot, rho, dst):
                    nc.vector.tensor_tensor(tmp[:, 2, :], bank[slot][:, :], work[:, 0, :], ALU.mult
                                            ).then_inc(taken, 1)
                    dve.wait_ge(swapped, rho + 1)
                    nc.vector.tensor_tensor(work2[:, 1, :], bank[5][:, :], work[:, 1, :], ALU.mult
                                            ).then_inc(rot_b, 1)
                    dve.wait_ge(taken, b + 1)
                    dve.wait_ge(rot_b, rho + 1)
                    nc.vector.tensor_tensor(dst, tmp[:, 2, :], work2[:, 1, :], ALU.add).then_inc(rotated, 1)

                def finish(j):
                    b, slot = B + j, (B + j) % RING
                    rt = tmp[:, j % 2, :]
                    if j == 2:
                        dve.wait_ge(kc_rows, 16 * a + 4)
                    if j == 3:
                        dve.wait_ge(kc_rows, 16 * a + 8)
                    if j in (4, 5):
                        dve.wait_ge(kc_rows, 16 * a + 4 * (j - 1))
                    if j in (6, 7):
                        dve.wait_ge(key_hi_ready, 16 * a + 4 * (j - 5))
                    if j in (VC, VC + 1):
                        dve.wait_ge(block_done, b + 1)
                        nc.vector.tensor_tensor(rt, bank[slot][:, :], rrow, ALU.mult).then_inc(taken, 1)
                        return
                    rho = 14 * a + (j if j < 2 else j - 2)
                    if rho:
                        dve.wait_ge(rotated, rho)
                    rotate(b, slot, rho, rt)
                    if j >= KS:
                        r = (j - KS) // 2
                        dve.wait_ge(rotated, rho + 1)
                        for half in range(2):
                            g = 2 * (j % 2) + half
                            src = rt[64 * half:64 * half + 64, :]
                            dve.wait_ge(key_hi_ready, 16 * a + 4 * (j - 4) + 2 * half + 1)
                            for h in (half, 1 - half):
                                nc.vector.tensor_tensor(key_lo[64 * h:64 * h + 64, r, g, :], src,
                                                        f32(key_hi[64 * half:64 * half + 64, r, g, :]),
                                                        ALU.subtract).then_inc(key_lo_ready, 1)

                def cm(c):
                    v = c // 4
                    dve.wait_ge(cm_full, 8 * a + c + 1)
                    dve.wait_ge(cm_hi_ready, 8 * a + c + 1)
                    nc.vector.tensor_tensor(cm_lo[:, v, bass.ts(c % 4, S)], tmp[:, 3, :],
                                            f32(cm_hi[:, v, bass.ts(c % 4, S)]), ALU.subtract
                                            ).then_inc(cm_lo_ready, 1)

                sum_split(n)
                for v in range(2):
                    nc.vector.memset(kc2[:, v, :, S - 1:KCW], 0.0).then_inc(kc_pad, 1)
                for j in range(W1K):
                    b, slot = B + j, (B + j) % RING
                    split_after(b, slot)
                    if j == 0:
                        norm(n)
                        dve.wait_ge(rope_sin, 2)
                        for i in range(2):
                            nc.vector.tensor_tensor(work[:, i, :], rope[:, i, :], rrow, ALU.mult
                                                    ).then_inc(tab_ready, 1)
                        dve.wait_ge(tab_ready, 2 * (a + 1))
                    if j not in (VC, VC + 1):
                        rope_low(b, slot, 14 * a + (j if j < 2 else j - 2))
                    if j:
                        finish(j - 1)
                    if j >= 4:
                        cm(j - 4)
                finish(W1K - 1)
                for j in range(W1K, W2):
                    b, slot = B + j, (B + j) % RING
                    split_after(b, slot)
                    if j < W1K + 4:
                        cm(j - W1K + 4)
                    if j % 2:
                        q = (j - W1K) // 2
                        dve.wait_ge(ch_hi_ready, 4 * a + q + 1)
                        nc.vector.tensor_tensor(ch_lo[:, q, :], tmp[:, 2, bass.ts(q, P)], f32(ch_hi[:, q, :]),
                                                ALU.subtract).then_inc(taken, 2)
                b, slot = B + W2, (B + W2) % RING
                split_after(b, slot)
                dve.wait_ge(kcmp_hi, a + 1)
                dve.wait_ge(vcmp_hi, a + 1)
                nc.vector.tensor_tensor(vc_lo[:, :], vc_f, f32(vc_hi[:, :]), ALU.subtract
                                        ).then_inc(vcmp_lo, 1)
                nc.vector.tensor_tensor(kc_lo[:, :], bank[slot][:, 0:P], f32(kc_hi[:, :]), ALU.subtract
                                        ).then_inc(taken, 1)
                with dve.Fori(0, 2) as i:
                    for k in range(RING):
                        slot = (B + Q + k) % RING
                        b, rho = i * RING + (B + Q + k), i * RING + (14 * a + 6 + k)
                        split_after(b, slot)
                        rope_low(b, slot, rho)
                        if k:
                            dve.wait_ge(rotated, rho - 1)
                            rotate(b - 1, (slot - 1) % RING, rho - 1, tile(qf, i * RING + (k - 1)))
                    dve.wait_ge(rotated, rho)
                    rotate(b, slot, rho, tile(qf, i * RING + (RING - 1)))
                b, slot = B + GATE, (B + GATE) % RING
                split_after(b, slot)
                dve.wait_ge(block_done, b + 1)
                nc.vector.tensor_copy(work2[:, 0, :], bank[slot][:, :]).then_inc(taken, 1)
                for j in range(4):
                    split_after(B + V + j, (B + V + j) % RING)
                dve.wait_ge(block_done, B + V + 4)
                for t in range(TT):
                    nc.vector.tensor_scalar(val[:, t, :], bank[(B + V + t) % RING][:, :], rcol[:, t, 0:1], None,
                                            ALU.mult).then_inc(taken, 1)
                dve.wait_ge(gate_ready, 4 * (a + 1))
                nc.vector.tensor_scalar(gates[:, 0, 0, :], gates[:, 0, 0, :], col("anyvalid", 0), None, ALU.mult
                                        ).then_inc(gate_masked, 1)
                dve.wait_ge(gate_masked, a + 1)
                attention(l, a)
                out_projection(l)

            def attention(l, a):
                def queries_low(g, t):
                    for h in range(2):
                        dve.wait_ge(q_hi_ready, g * 2 * TT + (8 * TT * a + 2 * t + h + 1))
                        nc.vector.scalar_tensor_tensor(
                            out=q_by_half[64 - 64 * h:128 - 64 * h, h, :, bass.ts(t, P)],
                            in0=qf[64 * h:64 * h + 64, bass.ds(g * 2, 2), bass.ts(t, P)], scalar=DH ** -0.5,
                            in1=f32(q_by_half[64 * h:64 * h + 64, h, :, bass.ts(t, P)]), op0=ALU.mult,
                            op1=ALU.subtract).then_inc(q_lo_ready, 1)

                def values_low(g, t):
                    for br in range(2):
                        dve.wait_ge(vs_hi_ready, g * 2 * TT + (8 * TT * a + 2 * t + br + 1))
                        v = val[:, t, bass.ds((g + 4 * br) * DH, DH)].unsqueeze(1).broadcast_to([P, 2, DH])
                        nc.vector.tensor_tensor(vs_lo[:, t, br, :, :], v, f32(vs_hi[:, t, br, :, :]), ALU.subtract
                                                ).then_inc(vs_lo_ready, 1)

                def maximum(g, s):
                    u = g * UNITS + (TT * UNITS * a + s)
                    width = P if s % 9 == 0 else P * (s // 9 + 1)
                    dve.wait_ge(score_ready, u + 1)
                    if s % 9 == 0:
                        sc = bank[s % 2][:, 0:P].rearrange("p (j n) -> p j n", j=4)
                        nc.vector.tensor_reduce(nmax[:, s % 4, :], sc, AX.X, ALU.max, negate=True
                                                ).then_inc(cmax_ready, 1)
                        dve.wait_ge(cmax_ready, g * TT + (16 * a + s // 9 + 1))
                        wait_past(dve, prob_t, u - 3)
                        nc.vector.tensor_tensor(
                            prob[s % 4][:, 0:P].rearrange("p (j n) -> p j n", j=4), sc,
                            nmax[:, s % 4, :].unsqueeze(2).broadcast_to([P, 4, NCMP]), ALU.add
                        ).then_inc(max_ready, 1)
                    else:
                        nc.vector.tensor_reduce(nmax[:, s % 4, 0:1], bank[s % 2][:, 0:width], AX.X,
                                                ALU.max, negate=True).then_inc(max_ready, 1)

                def one_over_sums(g, x):
                    dve.wait_ge(prob_ready, g * UNITS + (TT * UNITS * a + x + 1))
                    if x % 9 == 0:
                        e = g * TT + (16 * a + x // 9)
                        wait_past(dve, cwgt_ready, e)
                        nc.vector.tensor_reduce(
                            cden[:, 0, :], prob[x % 4][:, 0:P].rearrange("p (j n) -> p j n", j=4),
                            AX.X, ALU.add).then_inc(csum_ready, 1)
                        dve.wait_ge(csum_ready, e + 1)
                        nc.vector.reciprocal(cden[:, 0, :], cden[:, 0, :]).then_inc(recip_ready, 1)
                    else:
                        d = den[:, x % 4:x % 4 + 1]
                        nc.vector.reciprocal(d, d).then_inc(recip_ready, 1)

                def weights(g, x):
                    t, r = x % UNITS // 9, x % 9
                    dve.wait_ge(recip_ready, g * UNITS + (TT * UNITS * a + x + 1))
                    if r == 0:
                        nc.vector.tensor_tensor(cden[:, 1, :], gates[:, t, 0, bass.ds(g * 4, 4)],
                                                cden[:, 0, :], ALU.mult).then_inc(cwgt_ready, 1)
                        dve.wait_ge(cwgt_ready, g * TT + (16 * a + t + 1))
                        pc = prob[x % 4][:, 0:P].rearrange("p (j n) -> p j n", j=4)
                        nc.vector.tensor_tensor(pc, pc, cden[:, 1, :].unsqueeze(2).broadcast_to([P, 4, NCMP]),
                                                ALU.mult).then_inc(diag_ready, 1)
                    else:
                        head = g * 4 + ((r - 1) % 4 + 4 * (x // UNITS))
                        gate = gates[:, t, 1 + (r - 1) // 4, bass.ds(head, 1)]
                        nc.vector.tensor_scalar(diag[:, x % 4, :], ident[:, :], den[:, x % 4:x % 4 + 1], gate,
                                                ALU.mult, ALU.mult).then_inc(diag_ready, 1)

                def steps(g, begin, end, first):
                    for s in range(begin, end):
                        if s == 0:
                            if not first:
                                one_over_sums(g, -1)
                            queries_low(g, 0)
                        if s < UNITS:
                            maximum(g, s)
                        if s and ran(s - 1, first):
                            one_over_sums(g, s - 1)
                        c = pack_end(s - SPLIT)
                        if ran(s - SPLIT, first) and c is not None:
                            for i, w in pack_splits(c):
                                k = 2 * (c % 2) + i
                                dve.wait_ge(pt_hi_ready, g * SPLITS + (TT * SPLITS * a + splits_before(c) + i + 1))
                                nc.vector.tensor_tensor(pt_lo[:, k, 0:w], bank[2 + k][:, 0:w], f32(pt_hi[:, k, 0:w]),
                                                        ALU.subtract).then_inc(pt_lo_ready, 1)
                        if ran(s - 1, first):
                            weights(g, s - 1)
                        if s == 2:
                            dve.wait_ge(vcs_hi_ready, g * 4 + (16 * a + 4))
                            for j in range(4):
                                row = slice(NCMP * j, NCMP * j + NCMP)
                                vc = f32(vcr_lo[row, bass.ds(g, 1), :]).broadcast_to([NCMP, 2, DH])
                                nc.vector.tensor_copy(vcs_lo[row, j, :, :], vc).then_inc(vcs_lo_ready, 1)
                        if s == MULT:
                            values_low(g, 0)
                        if s % 9 == 5 and s < 9 * (TT - 1):
                            queries_low(g, s // 9 + 1)
                        if s % 9 == 8 and s < 9 * (TT - 1):
                            values_low(g, s // 9 + 1)
                        x = s - LEAVE
                        if ran(x, first) and x % 9 == 8:
                            t, tiles = x % UNITS // 9, bass.ds(g * 2 + 2 * (x // UNITS), 2)
                            for h in range(2):
                                dve.wait_ge(o_hi_ready, g * 2 * TT + (8 * TT * a + 2 * (x // 9) + h + 1))
                                half = slice(64 * h, 64 * h + 64)
                                nc.vector.tensor_tensor(
                                    mix_lo[half, tiles, bass.ts(t, P)],
                                    bank[6 + t % 2][half, :].rearrange("p (jj h q) -> p h jj q", jj=2, h=2)[:, h, :, :],
                                    f32(mix_hi[half, tiles, bass.ts(t, P)]), ALU.subtract
                                ).then_inc(o_lo_ready, 1)

                steps(0, 0, UNITS, True)
                with dve.Fori(1, GROUPS) as g:
                    steps(g, 0, UNITS, False)
                steps(GROUPS - 1, UNITS, UNITS + LEAVE, False)

            def sgu(l):
                B = plan.mix[l]
                sum_split(norm_of_mixer(l))
                for half in range(2):
                    for j in range(4):
                        b = B + 4 * half + j
                        split_after(b, b % RING)
                        if half == 0 and j == 0:
                            norm(norm_of_mixer(l))
                    if half:
                        slot = (B + SGU_WS) % RING
                        low = tril[:, :].unsqueeze(1).broadcast_to([P, 8, P])
                        dve.wait_ge(w_lo_ready, B + SGU_WS + 1)
                        for dst, src in ((ws_hi, w_hi), (ws_lo, w_lo)):
                            nc.vector.tensor_tensor(
                                dst.rearrange("p (g t) -> p g t", g=8),
                                f32(src[:, slot, :]).rearrange("p (g t) -> p g t", g=8), low, ALU.mult
                            ).then_inc(ws_masked, 1)
                    for t in range(TT):
                        dve.wait_ge(v_gelu, 4 * half + t + 1)
                        nc.vector.bn_stats(bnst[:, t, half, :], sgu_v[:, t, bass.ts(half, S)]).then_inc(taken, 1)
                split_after(B + SGU_WS, (B + SGU_WS) % RING)
                dve.wait_ge(taken, B + 8)
                for t in range(TT):
                    nc.vector.bn_aggr(mv[:, t, :], bnst[:, t, :, :].rearrange("p a b -> p (a b)")).then_inc(ln_step, 1)
                dve.wait_ge(ln_step, TT)
                nc.vector.tensor_scalar(lstd[:, 0, :], mv[:, :, 1], LN_EPS, None, ALU.add).then_inc(ln_var, 1)
                dve.wait_ge(ln_std, 1)
                rsqrt_steps(lstd[:, 0, :], lstd[:, 1, :], lstd[:, 2, :], ln_step, TT)
                for t in range(TT):
                    nc.vector.tensor_scalar(sgu_v[:, t, :], sgu_v[:, t, :], mv[:, t, 0:1], lstd[:, 1, t:t + 1],
                                            ALU.subtract, ALU.mult).then_inc(vn_ready, 1)
                    dve.wait_ge(vn_hi, t + 1)
                    nc.vector.tensor_tensor(v_lo[:, t, :], sgu_v[:, t, :], f32(v_hi[:, t, :]), ALU.subtract
                                            ).then_inc(vn_lo, 1)
                    if t < 3:
                        split_after(B + SGU_U + t, (B + SGU_U + t) % RING)
                dve.wait_ge(block_done, B + SGU_WS + 1)
                dve.wait_ge(bs_full, 16)
                for g in range(8):
                    nc.vector.scalar_tensor_tensor(
                        out=bias_t[:, bass.ts(g, P)], in0=bank[4 + g // 4][:, bass.ts(g % 4, P)],
                        scalar=col("ln_b", g), in1=bs_t[:, bass.ts(g, P)], op0=ALU.mult, op1=ALU.add
                    ).then_inc(bias_ready if g < 7 else taken, 1)
                for m in range(MT):
                    b = B + SGU_U + m
                    if m + 3 < MT:
                        split_after(b + 3, (b + 3) % RING)
                    dve.wait_ge(block_done, b + 1)
                    nc.vector.tensor_tensor(tmp[:, 0, :], bank[b % RING][:, :], rrow, ALU.mult).then_inc(taken, 1)
                    dve.wait_ge(mixed, m + 1)
                    dve.wait_ge(taken, B + SGU_U)
                    nc.vector.scalar_tensor_tensor(
                        out=tmp[:, 2, :].rearrange("p (n t) -> p n t", n=TT),
                        in0=bank[6 + m % 2][:, :].rearrange("p (n t) -> p n t", n=TT), scalar=col("ln_g", m),
                        in1=bias_t[:, bass.ts(m, P)].unsqueeze(1).broadcast_to([P, TT, P]),
                        op0=ALU.mult, op1=ALU.add).then_inc(sv_ready, 1)
                    dve.wait_ge(sv_ready, m + 1)
                    dve.wait_ge(u_gelu, m + 1)
                    nc.vector.tensor_tensor(tmp[:, 3, :], tmp[:, 1, :], tmp[:, 2, :], ALU.mult).then_inc(mix_full, 1)
                    dve.wait_ge(mix_full, m + 1)
                    dve.wait_ge(mix_hi_ready, m + 1)
                    nc.vector.tensor_tensor(mix_lo[:, m, :], tmp[:, 3, :], f32(mix_hi[:, m, :]), ALU.subtract
                                            ).then_inc(mix_lo_ready, 1)
                out_projection(l)

            def pool(l):
                B = plan.mix[l]
                width = POOL_PAD + S
                bufs = [big[:, i * width:(i + 1) * width] for i in range(3)]
                sum_split(norm_of_mixer(l))
                for z in bufs:
                    nc.vector.memset(z[:, 0:POOL_PAD], 0.0).then_inc(z_pad, 1)
                steps = 0
                for m in range(MT):
                    b = B + m
                    split_after(b, b % RING)
                    if m == 0:
                        norm(norm_of_mixer(l))
                        dve.wait_ge(z_pad, 3)
                    gi = m // 2
                    dve.wait_ge(block_done, b + 1)
                    nc.vector.tensor_tensor(bufs[0][:, POOL_PAD:], bank[b % RING][:, :], rrow, ALU.mult
                                            ).then_inc(taken, 1)
                    dve.wait_ge(taken, b + 1)
                    cur = bufs[0]
                    for s in range(gi + 1):
                        nxt = bufs[1 + s % 2]
                        nc.vector.tensor_tensor(nxt[:, POOL_PAD:], cur[:, POOL_PAD:],
                                                cur[:, POOL_PAD - 2 ** s:width - 2 ** s], ALU.add
                                                ).then_inc(pool_step, 1)
                        steps += 1
                        dve.wait_ge(pool_step, steps)
                        cur = nxt
                    head = cur[:, POOL_PAD:2 * POOL_PAD]
                    at = PAR["corr"] + gi * POOL_PAD
                    nc.vector.tensor_tensor(head, head, par[:, at:at + POOL_PAD], ALU.mult).then_inc(pool_step, 1)
                    steps += 1
                    dve.wait_ge(pool_step, steps)
                    nc.vector.scalar_tensor_tensor(out=tmp[:, 3, :], in0=cur[:, POOL_PAD:], scalar=0.5 ** (gi + 1),
                                                   in1=bufs[0][:, POOL_PAD:], op0=ALU.mult, op1=ALU.subtract
                                                   ).then_inc(d_full, 1)
                    dve.wait_ge(d_full, m + 1)
                    dve.wait_ge(d_hi, m + 1)
                    nc.vector.tensor_tensor(hid_lo[:, m, :], tmp[:, 3, :], f32(hid_hi[:, m, :]), ALU.subtract
                                            ).then_inc(d_lo, 1)
                for i in range(2):
                    b = B + POOL_GRP + i
                    split_after(b, b % RING)
                    for q in range(4):
                        m = 4 * i + q
                        dve.wait_ge(y_hi, m + 1)
                        nc.vector.scalar_tensor_tensor(
                            out=mix_lo[:, m, :], in0=bank[q][:, :], scalar=col("pool_scale", m),
                            in1=f32(mix_hi[:, m, :]), op0=ALU.mult, op1=ALU.subtract
                        ).then_inc(y_lo if q < 3 else taken, 1)
                out_projection(l)

            nc.vector.memset(f32(ones[:, :]), 1.0).then_inc(ones_ready, 1)
            split(0, 0)
            dve.wait_ge(par_full, 16)
            for m in range(MT):
                xs_low(0, m, m)
            for b in range(1, AHEAD):
                split(b, b)
            dve.wait_ge(pos_full, 16)
            ang, turn, aux = tmp[:, 3, :], tmp[:, 2, :], tmp[:, 0, :]
            def angle_step(i, ins):
                ins.then_inc(rope_step, 1)
                dve.wait_ge(rope_step, i)

            angle_step(1, nc.vector.tensor_copy(ang, tmp[:, 0, :].bitcast(I32)))
            angle_step(2, nc.vector.tensor_scalar(ang, ang, col("invf", 0), None, ALU.mult))
            angle_step(3, nc.vector.tensor_scalar(turn, ang, float(0.5 / np.pi), None, ALU.mult))
            angle_step(4, nc.vector.tensor_scalar(turn, turn, ROUND, None, ALU.add))
            angle_step(5, nc.vector.tensor_scalar(turn, turn, -ROUND, None, ALU.add))
            for i in range(3):
                angle_step(6 + i, nc.vector.scalar_tensor_tensor(out=ang, in0=turn, scalar=-TWO_PI[i], in1=ang,
                                                                 op0=ALU.mult, op1=ALU.add))
            angle_step(9, nc.vector.tensor_scalar(tmp[:, 1, :], ang, PI_F, -PI_F, ALU.min, ALU.max))
            angle_step(10, nc.vector.tensor_scalar(turn, ang, float(np.pi / 2), None, ALU.add))
            angle_step(11, nc.vector.tensor_scalar(aux, turn, float(np.pi), -2.0 * float(np.pi), ALU.is_gt,
                                                   ALU.mult))
            angle_step(12, nc.vector.tensor_tensor(turn, turn, aux, ALU.add))
            angle_step(13, nc.vector.tensor_scalar(turn, turn, PI_F, -PI_F, ALU.min, ALU.max))
            dve.wait_ge(con_ready, 6)
            dve.wait_ge(rope_sin, 2)
            a = 0
            for l, (kind, _) in enumerate(plan.mixers):
                if kind == "nsa":
                    nsa(l, a)
                    a += 1
                elif kind == "sgu":
                    sgu(l)
                else:
                    pool(l)
                ffn(l)
            n = plan.norms - 1
            sum_split(n)
            norm(n)
            for m in range(MT):
                nc.vector.scalar_tensor_tensor(out=qf[:, m, :], in0=x[:, m, :], scalar=g_of(n, m), in1=rrow,
                                               op0=ALU.mult, op1=ALU.mult).then_inc(y_out, 1)

        @block.tensor
        def _(pe):
            def mm(out_, w, v, start, stop):
                return nc.tensor.matmul(out_, w, v, start=start, stop=stop)

            def mm3(out_, w, v, start, stop):
                mm(out_, w[0], v[0], start, False)
                mm(out_, w[0], v[1], False, False)
                return mm(out_, w[1], v[0], False, stop)

            def wslot(slot, at, n=P):
                return w_hi[:, slot, at:at + n], w_lo[:, slot, at:at + n]

            def open_block(b):
                pe.wait_ge(w_lo_ready, b + 1)
                if not (type(b) is int and b < RING):
                    pe.wait_ge(taken, b - RING + 1)

            def project(b, slot, nk, mov, ready=None):
                open_block(b)
                for k in range(nk):
                    if ready is not None:
                        pe.wait_ge(ready[0], ready[1] + k + 1)
                    last = mm3(bank[slot][:, :], wslot(slot, k * P), mov(k), k == 0, k == nk - 1)
                last.then_inc(block_done, 1)

            xs = lambda k: (xs_hi[:, k, :], xs_lo[:, k, :])
            hid = lambda k: (hid_hi[:, k, :], hid_lo[:, k, :])
            mix = lambda k: (mix_hi[:, k, :], mix_lo[:, k, :])

            def norm(n):
                pe.wait_ge(sq_lo_ready, n + 1)
                if n == 0:
                    pe.wait_ge(ones_ready, 1)
                mm(bank[4][:, :], ones[:, :], sq_hi, True, False)
                mm(bank[4][:, :], ones[:, :], sq_lo, False, True)
                for t in range(TT):
                    mm(bank[5][:, 2 * t:2 * t + 2], sq_hi[:, bass.ts(t, P)], ones[:, 0:2], True, False)
                    last = mm(bank[5][:, 2 * t:2 * t + 2], sq_lo[:, bass.ts(t, P)], ones[:, 0:2], False, True)
                last.then_inc(norm_sum, 1)

            def out_projection(l, ready=None):
                b0 = plan.out_block(l)
                s0 = b0 % RING
                with pe.Fori(0, MT // RING) as i:
                    for k in range(RING):
                        project(i * RING + (b0 + k), (s0 + k) % RING, MT, mix, ready if k == 0 else None)

            def ffn(l):
                n = norm_of_ffn(l)
                for p, tiles in enumerate(PARTS):
                    up, down = plan.part_block(l, p)
                    s0 = up % RING
                    t0 = HIDDEN_TILES * l + 8 * p
                    first = 0
                    if p == 0:
                        project(up, s0, MT, xs, (xs_lo_ready, MT * n))
                        norm(n)
                        for k in range(1, RING):
                            project(up + k, (s0 + k) % RING, MT, xs)
                        first = 1
                    with pe.Fori(first, tiles // 2) as i:
                        for k in range(RING):
                            project(i * RING + (up + k), (s0 + k) % RING, MT, xs)
                    s0d = down % RING
                    with pe.Fori(0, MT // RING) as i:
                        for k in range(RING):
                            project(i * RING + (down + k), (s0d + k) % RING, tiles, hid,
                                    (hid_lo_ready, t0) if k == 0 else None)

            def swap_rows(rho):
                pe.wait_ge(rq_lo_ready, rho + 1)
                if not (type(rho) is int and rho == 0):
                    pe.wait_ge(rot_b, rho)
                mm(bank[5][:, :], swap[:, :], sq_hi, True, False)
                mm(bank[5][:, :], swap[:, :], sq_lo, False, True).then_inc(swapped, 1)

            def values(b0, banks, free, amid=None):
                pe.wait_ge(taken, free)
                for j in range(4):
                    pe.wait_ge(w_lo_ready, b0 + j + 1)
                    for kk in range(2):
                        k = 2 * j + kk
                        for t in range(TT):
                            x_t = (xs_hi[:, k, bass.ts(t, P)], xs_lo[:, k, bass.ts(t, P)])
                            last = mm3(bank[banks[t]][:, :], x_t, wslot((b0 + j) % RING, kk * S, S), k == 0, k == 7)
                    last.then_inc(block_done, 1)
                    if j == 1 and amid is not None:
                        amid()

            def nsa(l, a):
                B = plan.mix[l]
                n = norm_of_mixer(l)
                for j in range(W1K):
                    project(B + j, (B + j) % RING, MT, xs, (xs_lo_ready, MT * n) if j == 0 else None)
                    if j == 0:
                        norm(n)
                        if a == 0:
                            pe.wait_ge(con_ready, 6)
                    if j and j - 1 not in (VC, VC + 1):
                        swap_rows(14 * a + (j - 1 if j - 1 < 2 else j - 3))
                swap_rows(14 * a + 5)
                for j in range(W1K, W2):
                    b, slot = B + j, (B + j) % RING
                    v, half = (j - W1K) // 4, j % 2
                    open_block(b)
                    dst = bank[slot if not half else (slot - 1) % RING][:, 0:P]
                    for k in range(8):
                        kt = 8 * half + k
                        if kt % 4 == 0:
                            pe.wait_ge(cm_lo_ready, 8 * a + 4 * v + kt // 4 + 1)
                        last = mm3(dst, wslot(slot, k * P), (cm_hi[:, v, bass.ts(kt, P)], cm_lo[:, v, bass.ts(kt, P)]),
                                   kt == 0, kt == 15)
                    last.then_inc(block_done, 1)
                b, slot = B + W2, (B + W2) % RING
                open_block(b)
                pe.wait_ge(taken, b)
                for q in range(2):
                    mm3(bank[slot][:, 0:P], wslot(slot, q * P), (ch_hi[:, q, :], ch_lo[:, q, :]), q == 0, q == 1)
                for q in range(2):
                    last = mm3(bank[6][:, 0:DH], (ch_hi[:, 2 + q, :], ch_lo[:, 2 + q, :]),
                               wslot(slot, 2 * P + q * DH, DH), q == 0, q == 1)
                last.then_inc(block_done, 1)
                with pe.Fori(0, 2) as i:
                    for k in range(RING):
                        project(i * RING + (B + Q + k), (B + Q + k) % RING, MT, xs)
                        if k:
                            swap_rows(i * RING + (14 * a + 6 + k - 1))
                    swap_rows(i * RING + (14 * a + 6 + RING - 1))
                project(B + GATE, (B + GATE) % RING, MT, xs)

                def turn_gates():
                    for t in range(TT):
                        last = nc.tensor.transpose(bank[6][:, bass.ts(t, P)], work2[:, 0, bass.ts(t, P)], ident[:, :])
                    last.then_inc(gate_turned, 1)

                values(B + V, [(B + V + t) % RING for t in range(TT)], B + V, turn_gates)
                attention(l, a)
                out_projection(l)

            def attention(l, a):
                pe.wait_ge(taken, plan.mix[l] + NSA_OUT)
                pe.wait_ge(key_hi_ready, 16 * (a + 1))
                pe.wait_ge(key_lo_ready, 16 * (a + 1))

                def scores(g, s):
                    t, r = s // 9, s % 9
                    dst = bank[s % 2]
                    u = g * UNITS + (TT * UNITS * a + s)
                    wait_past(pe, prob_ready, u - 1)
                    if r == 0:
                        pe.wait_ge(q_lo_ready, g * 2 * TT + (8 * TT * a + 2 * (t + 1)))
                        mm(dst[:, 0:P], ident_b[:, :], cmask_b[:, t, :], True, False)
                        for j in range(4):
                            q = q_st[:, j, bass.ts(t, P)]
                            mm(dst[:, bass.ts(j, NCMP)], q, kc_hi[:, bass.ds(g * NCMP, NCMP)], False, False)
                            last = mm(dst[:, bass.ts(j, NCMP)], q, kc_lo[:, bass.ds(g * NCMP, NCMP)], False, j == 3)
                    else:
                        br, j = (r - 1) // 4, (r - 1) % 4
                        q = q_st[:, j, bass.ts(t, P)]
                        width = P * (t + 1)
                        keys = [k[:, br, bass.ds(g, 1), 0:width].rearrange("p o t -> p (o t)")
                                for k in (key_hi, key_lo)]
                        mm(dst[:, 0:width], q, keys[0], True, False)
                        mm(dst[:, 0:width], q, keys[1], False, False)
                        last = mm(dst[:, bass.ts(t, P)], ident_b[:, :], causal_b[:, :], False, True)
                    last.then_inc(score_ready, 1)

                def turn(g, s):
                    t, r = s % UNITS // 9, s % 9
                    c = 5 * (s // 9) + (r + 1) // 2
                    pe.wait_ge(diag_ready, g * UNITS + (TT * UNITS * a + s + 1))
                    if r == 0 or r % 2:
                        wait_past(pe, pt_lo_ready, g * SPLITS + (TT * SPLITS * a + splits_before(c - 1)))
                    if r == 0:
                        last = nc.tensor.transpose(bank[2 + 2 * (c % 2)][:, 0:P], prob[s % 4][:, 0:P], ident[:, :])
                    else:
                        for kb in range(t + 1):
                            at = 2 * P * (kb % 2) + P * ((r - 1) % 2)
                            last = mm(bank[2 + 2 * (c % 2) + kb // 2][:, at:at + P], prob[s % 4][:, bass.ts(kb, P)],
                                      diag[:, s % 4, :], True, True)
                    last.then_inc(prob_t, 1)

                def products(g, c):
                    t, p = c % PACKS // 5, c % 5
                    k = 2 * (c % 2)
                    pe.wait_ge(pt_lo_ready, g * SPLITS + (TT * SPLITS * a + splits_before(c + 1)))
                    if p == 0:
                        wait_past(pe, o_lo_ready, g * 2 * TT + (8 * TT * a + 2 * (c // 5 - 1)))
                        if t == 0:
                            pe.wait_ge(vcs_lo_ready, g * 4 + (16 * a + 4))
                        for j in range(4):
                            v = [m[:, j, :, :].rearrange("p h d -> p (h d)") for m in (vcs_hi, vcs_lo)]
                            last = mm3(bank[6 + t % 2][:, bass.ts(j, P)], v, (pt_hi[:, k, 0:P], pt_lo[:, k, 0:P]),
                                       j == 0, False)
                    else:
                        br, pair = (p - 1) // 2, (p - 1) % 2
                        if p == 1:
                            pe.wait_ge(vs_lo_ready, g * 2 * TT + (8 * TT * a + 2 * (c // 5 + 1)))
                        for kb in range(t + 1):
                            v = [m[:, kb, br, :, :].rearrange("p h d -> p (h d)") for m in (vs_hi, vs_lo)]
                            pt = [m[:, k + kb // 2, bass.ts(kb % 2, 2 * P)] for m in (pt_hi, pt_lo)]
                            last = mm3(bank[6 + t % 2][:, bass.ts(pair, 2 * P)], v, pt, False, br == 1 and pair == 1 and kb == t)
                    last.then_inc(pv_done, 1)

                def steps(g, begin, end, first):
                    for s in range(begin, end):
                        if 0 < s < UNITS:
                            scores(g, s)
                        if ran(s - TURN, first):
                            turn(g, s - TURN)
                        if ran(s - MULT, first) and pack_end(s - MULT) is not None:
                            products(g, pack_end(s - MULT))
                        if s == 0:
                            scores(g, s)

                steps(0, 0, UNITS, True)
                with pe.Fori(1, GROUPS) as g:
                    steps(g, 0, UNITS, False)
                steps(GROUPS - 1, UNITS, UNITS + MULT, False)
                pe.wait_ge(o_lo_ready, 8 * TT * (a + 1))

            def sgu(l):
                B = plan.mix[l]
                n = norm_of_mixer(l)
                for k in range(MT):
                    pe.wait_ge(xs_lo_ready, MT * n + k + 1)
                norm(n)
                for half in range(2):
                    values(B + 4 * half, [(B + t) % RING for t in range(TT)], B + 4 * half)
                b = B + SGU_WS
                pe.wait_ge(ws_masked, 2)
                for h in range(2):
                    mm(bank[4 + h][:, :], ones[:, :], ws_hi[:, bass.ts(h, S)], True, False)
                    last = mm(bank[4 + h][:, :], ones[:, :], ws_lo[:, bass.ts(h, S)], False, True)
                last.then_inc(block_done, 1)
                for m in range(MT + 3):
                    if m >= 3:
                        q = m - 3
                        if q == 0:
                            pe.wait_ge(vn_lo, TT)
                        if q >= 2:
                            pe.wait_ge(sv_ready, q - 1)
                        for t in range(TT):
                            last = mm3(bank[6 + q % 2][:, bass.ts(t, P)],
                                       (v_hi[:, t, bass.ts(q, P)], v_lo[:, t, bass.ts(q, P)]),
                                       (ws_hi[:, bass.ts(q, P)], ws_lo[:, bass.ts(q, P)]), True, True)
                        last.then_inc(mixed, 1)
                    if m < MT:
                        project(B + SGU_U + m, (B + SGU_U + m) % RING, MT, xs)
                out_projection(l, (mix_lo_ready, 0))

            def pool(l):
                B = plan.mix[l]
                n = norm_of_mixer(l)
                for m in range(MT):
                    project(B + m, (B + m) % RING, MT, xs, (xs_lo_ready, MT * n) if m == 0 else None)
                    if m == 0:
                        norm(n)
                for i in range(2):
                    b = B + POOL_GRP + i
                    slot = b % RING
                    pe.wait_ge(w_lo_ready, b + 1)
                    if i == 0:
                        pe.wait_ge(taken, b)
                    for q in range(4):
                        if i:
                            if q < 3:
                                pe.wait_ge(y_lo, q + 1)
                            else:
                                pe.wait_ge(taken, b)
                        for c in range(2):
                            k = 2 * (2 * i + q // 2) + c
                            pe.wait_ge(d_lo, k + 1)
                            last = mm3(bank[q][:, :], wslot(slot, (2 * q + c) * P), hid(k), c == 0, c == 1)
                    last.then_inc(block_done, 1)
                pe.wait_ge(taken, B + POOL_OUT)
                pe.wait_ge(y_lo, 6)
                out_projection(l)

            a = 0
            for l, (kind, _) in enumerate(plan.mixers):
                if kind == "nsa":
                    nsa(l, a)
                    a += 1
                elif kind == "sgu":
                    sgu(l)
                else:
                    pool(l)
                ffn(l)
            norm(plan.norms - 1)


def _tiles(w, nk=MT):
    K, M = w.shape
    b = w.reshape(K // P, P, M // P, P).transpose(2, 1, 0, 3).reshape(M // P, P, (K // P) * P)
    return _pad(b)


def _pad(b):
    return np.pad(b, ((0, 0), (0, 0), (0, BW - b.shape[2]))) if b.shape[2] < BW else b


def _pairs(w):
    return w.reshape(4, 2, P, S).transpose(0, 2, 1, 3).reshape(4, P, BW)


def _stream(i, mixers, total):
    out = []
    for l, (kind, j) in enumerate(mixers):
        if kind == "nsa":
            w = i["nsa_w_in"][j]
            kc, vc, ks, vs, kw, vw = [w[:, D + 256 * n:D + 256 * (n + 1)] for n in range(6)]
            out += [_tiles(np.ascontiguousarray(c)) for c in (kc, vc, ks, kw)]
            for c in "kv":
                w1 = i[f"nsa_cmp_{c}_w1"][j].reshape(2, 8, P, 2, P)
                out.append(w1.transpose(3, 0, 2, 1, 4).reshape(4, P, BW))
            k2, v2 = (i[f"nsa_cmp_{c}_w2"][j].reshape(2, P, DH) for c in "kv")
            out.append(_pad(np.concatenate([k2[0], k2[0], k2[1], k2[1], v2[0], v2[1]], axis=1)[None]))
            out.append(_tiles(w[:, 0:D]))
            out.append(_tiles(np.pad(w[:, D + 1536:], ((0, 0), (0, P - 3 * HEADS)))))
            out.append(_pairs(np.concatenate([vs, vw], axis=1)))
            out.append(_tiles(i["nsa_w_out"][j]))
        elif kind == "sgu":
            w = i["sgu_w_in"][j]
            out += [_pairs(w[:, D + S * h:D + S * (h + 1)]) for h in range(2)]
            out.append(i["sgu_w_s"][j].transpose(2, 0, 1).reshape(1, P, BW))
            out.append(_tiles(w[:, 0:D]))
            out.append(_tiles(i["sgu_w_out"][j]))
        else:
            out.append(_tiles(i["pool_w_in"][j]))
            g = i["pool_w_grp"][j].reshape(2, 2, 2, P, 2, P)
            out.append(g.transpose(0, 3, 1, 4, 2, 5).reshape(2, P, BW))
            out.append(_tiles(i["pool_w_out"][j]))
        up, down = i["ffn_w_gate_up"][l], i["ffn_w_down"][l]
        gate, lin = (_tiles(up[:, h * HIDDEN_TILES * P:(h + 1) * HIDDEN_TILES * P]) for h in range(2))
        both = np.stack([gate, lin], axis=1)
        t = 0
        for n in PARTS:
            out.append(both[t:t + n].reshape(2 * n, P, BW))
            out.append(_tiles(down[t * P:(t + n) * P]))
            t += n
    have = sum(b.shape[0] for b in out)
    out.append(np.zeros((total - have, P, BW), np.float32))
    return np.concatenate(out)


def _params(i):
    par = np.zeros((P, PAR_COLS), np.float32)

    def put(name, v, at=0):
        par[:, PAR[name] + at:PAR[name] + at + v.shape[1]] = v

    def by_tile(v):
        return v.reshape(MT, P).T

    for n in range(4):
        put("gn", by_tile(i["mix_norm"][n]), 2 * n * MT)
        put("gn", by_tile(i["ffn_norm"][n]), (2 * n + 1) * MT)
    put("gn", by_tile(i["final_norm"]), 8 * MT)
    put("ln_g", by_tile(i["sgu_ln_g"][0]))
    put("ln_b", by_tile(i["sgu_ln_b"][0]))
    put("pool_scale", by_tile(i["pool_scale"][0]))
    for j in range(2):
        for v, c in enumerate("kv"):
            put("pos", i[f"nsa_cmp_pos_{c}"][j].reshape(16, P).T, 32 * j + 16 * v)
    d = np.arange(P) % DH
    half = ROPE_DIM // 2
    inv = ROPE_THETA ** (-np.arange(0, ROPE_DIM, 2, dtype=np.float64) / ROPE_DIM)
    put("invf", np.where(d < ROPE_DIM, inv[d % half], 0.0).astype(np.float32)[:, None])
    put("anyvalid", (np.arange(P) >= 31).astype(np.float32)[:, None])
    t = np.arange(POOL_PAD)
    for gi in range(4):
        w = 2 ** (gi + 1)
        put("corr", np.broadcast_to((w / np.minimum(t + 1, w)).astype(np.float32), (P, POOL_PAD)), gi * POOL_PAD)
    return par


def _consts():
    con = np.zeros((P, CON_COLS), np.float32)
    r = np.arange(P)
    con[:, CON["ident"]:CON["ident"] + P] = np.eye(P)
    half = ROPE_DIM // 2
    for h in (0, DH):
        for f in range(half):
            con[h + f + half, CON["swap"] + h + f] = -1.0
            con[h + f, CON["swap"] + h + f + half] = 1.0
    con[:, CON["causal"]:CON["causal"] + P] = np.where(r[None, :] > r[:, None], NEG, 0.0)
    con[:, CON["tril"]:CON["tril"] + P] = (r[None, :] >= r[:, None])
    n = np.arange(P) % NCMP
    for t in range(TT):
        ok = (16 * n[None, :] + 31 <= P * t + r[:, None]) & (n[None, :] < 31)
        con[:, CON["cmask"] + P * t:CON["cmask"] + P * (t + 1)] = np.where(ok, 0.0, NEG)
    return con


def kernel(mixers=MIXERS, **inputs):
    import concourse.bacc as bacc
    from concourse.bass_utils import run_bass_kernel_spmd

    i = {k: np.asarray(v) for k, v in inputs.items()}
    plan = Plan(mixers)
    arrays = {
        "x_in": np.ascontiguousarray(i["x"][0].T.reshape(MT, P, S).transpose(1, 0, 2)),
        "positions": np.ascontiguousarray(i["positions"]),
        "stream": _stream(i, mixers, plan.stream),
        "params": _params(i),
        "consts": _consts(),
        "b_s": np.ascontiguousarray(i["sgu_b_s"][0].reshape(1, 8 * P)),
    }
    nc = bacc.Bacc("TRN2", target_bir_lowering=False, num_devices=1)
    args = [nc.dram_tensor(n, a.shape, mybir.dt.from_np(a.dtype), kind="ExternalInput").ap()
            for n, a in arrays.items()]
    out = nc.dram_tensor("out", (P, MT, S), F32, kind="ExternalOutput").ap()
    build(nc, *args, out, mixers=mixers)
    r = run_bass_kernel_spmd(nc, [arrays], core_ids=[0])
    y = r.results[0]["out"]
    return np.ascontiguousarray(y.transpose(1, 0, 2).reshape(D, S).T)[None]
```
